# Optimizing a Trainium2 kernel written in Bass

```python
import jax
import jax.numpy as jnp
from jax import lax
import numpy as np

D_MODEL = 2048
BATCH = 1
SEQ = 256
DEPTH = 2

D_MIX = D_MODEL
ATTN_HEAD_DIM = 64
ATTN_Q_HEADS = (D_MIX // 2) // ATTN_HEAD_DIM
ATTN_KV_HEADS = ATTN_Q_HEADS // 8
ATTN_Q_WIDTH = ATTN_Q_HEADS * ATTN_HEAD_DIM
ATTN_KV_WIDTH = ATTN_KV_HEADS * ATTN_HEAD_DIM
WINDOW = 128
ATTN_BLOCK = WINDOW
ROPE_THETA = 10000.0
HGRN_HEAD_DIM = 128
HGRN_HEADS = (D_MIX // 4) // HGRN_HEAD_DIM
HGRN_WIDTH = HGRN_HEADS * HGRN_HEAD_DIM
MLSTM_HEAD_DIM = 128
MLSTM_HEADS = (D_MIX // 4) // MLSTM_HEAD_DIM
MLSTM_WIDTH = MLSTM_HEADS * MLSTM_HEAD_DIM
MLSTM_CONV = 4
CHUNK = 64
IN_SIZES = (ATTN_Q_WIDTH, ATTN_KV_WIDTH, ATTN_KV_WIDTH,
            HGRN_WIDTH, HGRN_WIDTH, HGRN_WIDTH, HGRN_WIDTH,
            2 * MLSTM_WIDTH, MLSTM_WIDTH, MLSTM_WIDTH, MLSTM_HEADS, MLSTM_HEADS)
IN_DIM = sum(IN_SIZES)
MIX_OUT = ATTN_Q_WIDTH + HGRN_WIDTH + MLSTM_WIDTH
PEER_HEADS = 8
PEER_NKEYS = 128
PEER_EXPERTS = PEER_NKEYS * PEER_NKEYS
PEER_TOPK = 16
PEER_KEY_DIM = 256
PEER_TOKEN_BLOCK = 128
NORM_EPS = 1e-6
NEG_BIG = -1e30
TINY = 1e-30

kernel_name = "hymba_hgrn2_mlstm_swa_peer_trunk"

def rms_norm(x, g):
    xf = x.astype(jnp.float32)
    y = xf * lax.rsqrt(jnp.mean(xf * xf, axis=-1, keepdims=True) + NORM_EPS)
    return (y * g.astype(jnp.float32)).astype(x.dtype)

def split_cols(t, sizes):
    return jnp.split(t, np.cumsum(sizes)[:-1].tolist(), axis=-1)

def rotary(x, pos):
    half = x.shape[-1] // 2
    inv = ROPE_THETA ** (-jnp.arange(half, dtype=jnp.float32) / half)
    ang = pos.astype(jnp.float32)[:, None] * inv[None, :]
    cos = jnp.cos(ang)[None, :, None, :]
    sin = jnp.sin(ang)[None, :, None, :]
    xf = x.astype(jnp.float32)
    x1, x2 = xf[..., :half], xf[..., half:]
    return jnp.concatenate([x1 * cos - x2 * sin, x2 * cos + x1 * sin], axis=-1).astype(x.dtype)

def causal_depthwise_conv(x, w):
    k_width, s = w.shape[0], x.shape[1]
    xp = jnp.pad(x, ((0, 0), (k_width - 1, 0), (0, 0)))
    return sum(xp[:, j:j + s] * w[j] for j in range(k_width))

def to_chunks(t, c):
    b, s, h = t.shape[:3]
    t = t.reshape((b, s // c, c, h) + t.shape[3:])
    return jnp.moveaxis(t, (1, 3), (0, 2))

def from_chunks(t):
    t = jnp.moveaxis(t, (0, 2), (1, 3))
    b, n, c, h, d = t.shape
    return t.reshape(b, n * c, h, d)

def sliding_window_attention(q, k, v, sinks):
    b, s, hq, dh = q.shape
    hkv = k.shape[2]
    g = hq // hkv
    w = ATTN_BLOCK
    n = s // w
    qb = q.reshape(b, n, w, hkv, g, dh)

    def band(t):
        tb = t.reshape(b, n, w, hkv, dh)
        prev = jnp.pad(tb, ((0, 0), (1, 0), (0, 0), (0, 0), (0, 0)))[:, :-1]
        return jnp.concatenate([prev, tb], axis=2)

    kb, vb = band(k), band(v)
    logits = jnp.einsum('bnqhgd,bnkhd->bnhgqk', qb, kb).astype(jnp.float32) * (dh ** -0.5)
    qi = jnp.arange(w)[:, None]
    kj = jnp.arange(2 * w)[None, :]
    rel = qi + w - kj
    blk = jnp.arange(n)[:, None, None]
    valid = (rel >= 0) & (rel < WINDOW) & (blk * w - w + kj >= 0)
    logits = jnp.where(valid[None, :, None, None], logits, NEG_BIG)
    sink = jnp.broadcast_to(sinks.astype(jnp.float32).reshape(1, 1, hkv, g, 1, 1),
                            logits.shape[:-1] + (1,))
    probs = jax.nn.softmax(jnp.concatenate([logits, sink], axis=-1), axis=-1)[..., :-1]
    out = jnp.einsum('bnhgqk,bnkhd->bnqhgd', probs.astype(v.dtype), vb)
    return out.reshape(b, s, hq * dh)

def hgrn2_chunkwise(q, k, v, log_f):
    b, s, h, dk = q.shape
    dv = v.shape[-1]
    qc, kc, vc, ac = (to_chunks(t.astype(jnp.float32), CHUNK) for t in (q, k, v, log_f))
    causal = jnp.tril(jnp.ones((CHUNK, CHUNK), dtype=bool))[:, :, None]

    def step(state, inp):
        qi, ki, vi, ai = inp
        cum = jnp.cumsum(ai, axis=2)
        o_inter = jnp.einsum('bhtk,bhkv->bhtv', qi * jnp.exp(cum), state)
        rel = jnp.where(causal, cum[:, :, :, None, :] - cum[:, :, None, :, :], NEG_BIG)
        scores = jnp.einsum('bhtk,bhsk,bhtsk->bhts', qi, ki, jnp.exp(rel))
        o_intra = jnp.einsum('bhts,bhsv->bhtv', scores, vi)
        last = cum[:, :, -1]
        k_dec = ki * jnp.exp(last[:, :, None, :] - cum)
        state = jnp.exp(last)[..., None] * state + jnp.einsum('bhsk,bhsv->bhkv', k_dec, vi)
        return state, o_inter + o_intra

    init = jnp.zeros((b, h, dk, dv), jnp.float32)
    _, out = lax.scan(step, init, (qc, kc, vc, ac))
    return from_chunks(out)

def mlstm_chunkwise(q, k, v, i_pre, log_f):
    b, s, h, dk = q.shape
    dv = v.shape[-1]
    qc, kc, vc, ic, fc = (to_chunks(t.astype(jnp.float32), CHUNK) for t in (q, k, v, i_pre, log_f))
    causal = jnp.tril(jnp.ones((CHUNK, CHUNK), dtype=bool))

    def step(carry, inp):
        c_st, n_st, m = carry
        qi, ki, vi, ii, fi = inp
        cum = jnp.cumsum(fi, axis=-1)
        log_d = jnp.where(causal, cum[..., :, None] - cum[..., None, :] + ii[..., None, :], NEG_BIG)
        log_inter = cum + m[..., None]
        m_t = jnp.maximum(jnp.max(log_d, axis=-1), log_inter)
        w_intra = jnp.exp(log_d - m_t[..., None])
        w_inter = jnp.exp(log_inter - m_t)
        qk = jnp.einsum('bhtd,bhsd->bhts', qi, ki) * w_intra
        num = jnp.einsum('bhts,bhsv->bhtv', qk, vi) \
            + w_inter[..., None] * jnp.einsum('bhtd,bhdv->bhtv', qi, c_st)
        den = jnp.sum(qk, axis=-1) + w_inter * jnp.einsum('bhtd,bhd->bht', qi, n_st)
        h_out = num / jnp.maximum(jnp.abs(den), jnp.exp(-m_t))[..., None]
        last = cum[..., -1]
        log_w = last[..., None] - cum + ii
        m_new = jnp.maximum(last + m, jnp.max(log_w, axis=-1))
        w_s = jnp.exp(log_w - m_new[..., None])
        decay = jnp.exp(last + m - m_new)
        c_new = decay[..., None, None] * c_st + jnp.einsum('bhs,bhsd,bhsv->bhdv', w_s, ki, vi)
        n_new = decay[..., None] * n_st + jnp.einsum('bhs,bhsd->bhd', w_s, ki)
        return (c_new, n_new, m_new), h_out

    init = (jnp.zeros((b, h, dk, dv), jnp.float32), jnp.zeros((b, h, dk), jnp.float32),
            jnp.zeros((b, h), jnp.float32))
    _, out = lax.scan(step, init, (qc, kc, vc, ic, fc))
    return from_chunks(out)

def hybrid_mixer(h, w_in, w_out, sinks, lower_bound, hgrn_gain, conv_w, i_bias, f_bias):
    b, s, _ = h.shape
    pos = jnp.arange(s)
    (qa, ka, va, qh, fh, ih, gh, qkm, vm, om, im, fm) = split_cols(h @ w_in, IN_SIZES)

    qa = rotary(qa.reshape(b, s, ATTN_Q_HEADS, ATTN_HEAD_DIM), pos)
    ka = rotary(ka.reshape(b, s, ATTN_KV_HEADS, ATTN_HEAD_DIM), pos)
    va = va.reshape(b, s, ATTN_KV_HEADS, ATTN_HEAD_DIM)
    y_attn = sliding_window_attention(qa, ka, va, sinks)

    hs = (b, s, HGRN_HEADS, HGRN_HEAD_DIM)
    fz = fh.astype(jnp.float32)
    lb = lower_bound.astype(jnp.float32)
    f_gate = lb + (1.0 - lb) * jax.nn.sigmoid(fz)
    log_f = jnp.log(jnp.maximum(f_gate, TINY))
    k_h = (1.0 - lb) * jax.nn.sigmoid(-fz)
    o_h = hgrn2_chunkwise(jax.nn.silu(qh).reshape(hs), k_h.reshape(hs), ih.reshape(hs), log_f.reshape(hs))
    y_hgrn = rms_norm(o_h.astype(h.dtype), hgrn_gain.reshape(HGRN_HEADS, HGRN_HEAD_DIM))
    y_hgrn = y_hgrn.reshape(b, s, HGRN_WIDTH) * jax.nn.silu(gh)

    qk = jax.nn.silu(causal_depthwise_conv(qkm, conv_w))
    qm, km = jnp.split(qk, 2, axis=-1)
    ms = (b, s, MLSTM_HEADS, MLSTM_HEAD_DIM)
    o_m = mlstm_chunkwise(qm.reshape(ms), (km * MLSTM_HEAD_DIM ** -0.5).reshape(ms), vm.reshape(ms),
                          im + i_bias, jax.nn.log_sigmoid((fm + f_bias).astype(jnp.float32)))
    y_mlstm = jax.nn.sigmoid(om) * o_m.reshape(b, s, MLSTM_WIDTH).astype(h.dtype)

    y = jnp.concatenate([y_attn, y_hgrn, y_mlstm], axis=-1)
    return y @ w_out

def peer_ffn(x, w_query, sub_keys, expert_u, expert_v):
    b, s, d = x.shape
    xt = x.reshape(-1, d)
    t = xt.shape[0]
    q = (xt @ w_query).reshape(t, PEER_HEADS, 2, PEER_KEY_DIM // 2)
    s1 = jnp.einsum('thd,hnd->thn', q[:, :, 0], sub_keys[0]).astype(jnp.float32)
    s2 = jnp.einsum('thd,hnd->thn', q[:, :, 1], sub_keys[1]).astype(jnp.float32)
    v1, i1 = lax.top_k(s1, PEER_TOPK)
    v2, i2 = lax.top_k(s2, PEER_TOPK)
    cand = (v1[..., :, None] + v2[..., None, :]).reshape(t, PEER_HEADS, PEER_TOPK * PEER_TOPK)
    cidx = (i1[..., :, None] * PEER_NKEYS + i2[..., None, :]).reshape(t, PEER_HEADS, PEER_TOPK * PEER_TOPK)
    top_s, sel = lax.top_k(cand, PEER_TOPK)
    idx = jnp.take_along_axis(cidx, sel, axis=-1)
    gate = jax.nn.softmax(top_s, axis=-1)

    def block(args):
        xb, ib, gb = args
        pre = jnp.einsum('td,thkd->thk', xb, expert_u[ib])
        act = jax.nn.gelu(pre.astype(jnp.float32), approximate=False) * gb
        return jnp.einsum('thk,thkd->td', act.astype(xb.dtype), expert_v[ib])

    nb = t // PEER_TOKEN_BLOCK
    out = lax.map(block, (xt.reshape(nb, PEER_TOKEN_BLOCK, d),
                          idx.reshape(nb, PEER_TOKEN_BLOCK, PEER_HEADS, PEER_TOPK),
                          gate.reshape(nb, PEER_TOKEN_BLOCK, PEER_HEADS, PEER_TOPK)))
    return out.reshape(b, s, d)

def setup_inputs(seed: int = 0) -> dict:
    key = jax.random.key(seed)
    ks = jax.random.split(key, 17)

    def nrm(k, shape, scale):
        return jax.random.normal(k, shape, jnp.float32) * scale

    return {
        'x': nrm(ks[0], (BATCH, SEQ, D_MODEL), 1.0),
        'norm_mix': 1.0 + nrm(ks[1], (DEPTH, D_MODEL), 0.02),
        'w_in': nrm(ks[2], (DEPTH, D_MODEL, IN_DIM), D_MODEL ** -0.5),
        'w_out': nrm(ks[3], (DEPTH, MIX_OUT, D_MODEL), MIX_OUT ** -0.5),
        'attn_sinks': nrm(ks[4], (DEPTH, ATTN_Q_HEADS), 0.5),
        'hgrn_lb_logits': nrm(ks[5], (DEPTH, HGRN_WIDTH), 0.5),
        'hgrn_out_norm': 1.0 + nrm(ks[6], (DEPTH, HGRN_WIDTH), 0.02),
        'mlstm_conv': nrm(ks[7], (DEPTH, MLSTM_CONV, 2 * MLSTM_WIDTH), MLSTM_CONV ** -0.5),
        'mlstm_i_bias': nrm(ks[8], (DEPTH, MLSTM_HEADS), 0.1),
        'mlstm_f_bias': jnp.linspace(3.0, 6.0, MLSTM_HEADS, dtype=jnp.float32)[None, :]
                        + nrm(ks[9], (DEPTH, MLSTM_HEADS), 0.1),
        'norm_ffn': 1.0 + nrm(ks[10], (DEPTH, D_MODEL), 0.02),
        'peer_query': nrm(ks[11], (DEPTH, D_MODEL, PEER_HEADS * PEER_KEY_DIM), D_MODEL ** -0.5),
        'peer_sub_keys': nrm(ks[12], (DEPTH, 2, PEER_HEADS, PEER_NKEYS, PEER_KEY_DIM // 2),
                             (PEER_KEY_DIM // 2) ** -0.5),
        'peer_u': nrm(ks[13], (DEPTH, PEER_EXPERTS, D_MODEL), D_MODEL ** -0.5),
        'peer_v': nrm(ks[14], (DEPTH, PEER_EXPERTS, D_MODEL), PEER_TOPK ** -0.5),
        'norm_final': 1.0 + nrm(ks[15], (D_MODEL,), 0.02),
    }

def reference(x, norm_mix, w_in, w_out, attn_sinks, hgrn_lb_logits, hgrn_out_norm, mlstm_conv,
              mlstm_i_bias, mlstm_f_bias, norm_ffn, peer_query, peer_sub_keys, peer_u, peer_v,
              norm_final):
    p = jax.nn.softmax(hgrn_lb_logits.astype(jnp.float32), axis=0)
    lower_bounds = jnp.cumsum(p, axis=0) - p[0:1]
    for l in range(DEPTH):
        h = rms_norm(x, norm_mix[l])
        x = x + hybrid_mixer(h, w_in[l], w_out[l], attn_sinks[l], lower_bounds[l], hgrn_out_norm[l],
                             mlstm_conv[l], mlstm_i_bias[l], mlstm_f_bias[l])
        h = rms_norm(x, norm_ffn[l])
        x = x + peer_ffn(h, peer_query[l], peer_sub_keys[l], peer_u[l], peer_v[l])
    return rms_norm(x, norm_final)


_drawn_inputs = setup_inputs


def setup_inputs(seed=0):
    import zlib

    import numpy as np

    out = dict(_drawn_inputs(seed))
    spreads = {}
    factors = {'attn_sinks': 4.618,
     'hgrn_out_norm': 3.004,
     'mlstm_i_bias': 22.761,
     'norm_final': 7.534,
     'norm_ffn': 2.808}
    for name, (base, spread) in spreads.items():
        noise = np.random.default_rng([zlib.crc32(name.encode()), seed]).standard_normal(out[name].shape)
        drawn = base * np.exp(spread * noise) if base else spread * noise
        out[name] = jnp.asarray(drawn.astype(out[name].dtype))
    for name, factor in factors.items():
        out[name] = (out[name] * factor).astype(out[name].dtype)
    return out
```

```python
from contextlib import ExitStack

import numpy as np

import concourse.bass as bass
from concourse import mybir

ALU = mybir.AluOpType
ACT = mybir.ActivationFunctionType
F32 = mybir.dt.float32
U32 = mybir.dt.uint32
I32 = mybir.dt.int32
AX_X = mybir.AxisListType.X

P = 128
SEQ, D, DEPTH = 256, 2048, 2
NB = SEQ // P
NC = D // P
EPS, NEG, TINY = 1e-6, -1e30, 1e-30
DH, NQ, NKV = 64, 16, 2
NH = 4
CONV = 4
HEADS, NKEYS, TOPK = 8, 128, 16
EXPERTS = NKEYS * NKEYS
FLOOR = 2.0 ** -60

COLS = dict(qa=0, ka=1024, va=1152, qh=1280, fh=1792, ih=2304, gh=2816, qkm=3328, vm=4352, om=4864, gates=5376)
SLABS = [("fh", COLS["fh"], 512), ("qh", COLS["qh"], 512), ("qa0", 0, 512), ("qa1", 512, 512),
         ("kv", COLS["ka"], 256), ("qkm0", COLS["qkm"], 512), ("qkm1", COLS["qkm"] + 512, 512),
         ("ih", COLS["ih"], 512), ("vm", COLS["vm"], 512), ("gh", COLS["gh"], 512), ("om", COLS["om"], 512)]
NS = len(SLABS)
NO = D // 512
LEVELS = [64, 32, 16, 8, 4, 2, 1]
NL = len(LEVELS)
BATCHES = [(1, 0, 4), (1, 4, 4), (1, 8, 4), (1, 12, 4), (0, 0, 8), (0, 8, 8)]
NBATCH = len(BATCHES)
GROUPS = HEADS * NB
RING = 4

CONST = {}
_at = 0
for _name, _n in (("ident", P), ("causal", P), ("levels", NL * P), ("window", 2 * P), ("cos", NB * 32),
                  ("sin", NB * 32), ("pick", NH * P), ("iota", TOPK)):
    CONST[_name] = (_at, _at + _n)
    _at += _n
NCONST = _at


def constants():
    c = np.zeros((P, NCONST), np.float32)
    i, j = np.arange(P)[:, None], np.arange(P)[None, :]

    def put(name, value):
        a, b = CONST[name]
        c[:, a:b] = value

    put("ident", i == j)
    put("causal", i <= j)
    put("levels", np.concatenate([(i // (2 * L) == j // (2 * L)) & (i % (2 * L) < L) & (j % (2 * L) >= L)
                                  for L in LEVELS], axis=1))
    window = np.concatenate([np.where(j > i, 0.0, NEG), np.where(j <= i, 0.0, NEG)], axis=1)
    put("window", window)
    half = DH // 2
    inv = (np.float32(10000.0) ** (-np.arange(half, dtype=np.float32) / np.float32(half))).astype(np.float32)
    ang = (np.arange(SEQ, dtype=np.float32)[:, None] * inv[None, :]).astype(np.float32)
    for name, f in (("cos", np.cos), ("sin", np.sin)):
        put(name, f(ang.astype(np.float64)).reshape(NB, P, half).transpose(1, 0, 2).reshape(P, NB * half))
    a, _ = CONST["pick"]
    for h in range(NH):
        c[h, a + h * P:a + (h + 1) * P] = 1.0
    put("iota", np.arange(TOPK)[None, :])
    return c


class Signal:

    def __init__(self, sem, per_layer, start=0):
        self.sem, self.per_layer, self.start = sem, per_layer, start

    def upto(self, layer, n):
        return layer * self.per_layer + (n + self.start)


def trunk(nc, x, norm_mix, w_in, w_out, attn_sinks, hgrn_lb_logits, hgrn_out_norm, mlstm_conv, mlstm_i_bias,
          mlstm_f_bias, norm_ffn, peer_query, peer_sub_keys, peer_u, peer_v, norm_final, consts, out):
    with ExitStack() as ctx:
        def sb(name, shape, dt=F32):
            return ctx.enter_context(nc.sbuf_tensor(name, shape, dt))

        def signal(name, per_layer, start=0):
            return Signal(ctx.enter_context(nc.semaphore(name)), per_layer, start)

        cst = sb("cst", [P, NCONST])
        xs = sb("xs", [P, NB, D])
        hn = sb("hn", [P, NB, D])
        hT = sb("hT", [P, NC, SEQ])
        slab = [sb(f"slab{i}", [P, NC * 512]) for i in range(2)]
        keysT = sb("keysT", [P, 2 * HEADS, NKEYS])
        gain = sb("gain", [P, D])
        work = sb("work", [P, 4 * NC * 256])
        PS = ctx.enter_context(nc.psum_tensor("PS", [P, 8, 512], F32))

        ones = sb("ones", [P, P])
        diag = sb("diag", [P, RING, P])
        gates_w = sb("gates_w", [P, NC, 2 * NH])
        lb_rows = sb("lb_rows", [DEPTH * NH, P])
        conv_rows = sb("conv_rows", [CONV * 2 * NH, P])
        conv_w = sb("conv_w", [P, CONV, 2 * NH])
        lb_all = sb("lb_all", [P, 2, DEPTH, NH])
        lb = sb("lb", [P, 2, NH])
        lbt = sb("lbt", [P, 4, NH])
        sinks = sb("sinks", [P, 1, NQ])
        sinks8 = sb("sinks8", [P, NQ])
        gate_bias = sb("gate_bias", [P, 1, 2 * NH])
        ss = sb("ss", [P, NB])
        rms = sb("rms", [P, NB])
        rstd = sb("rstd", [P, NB])
        mx = sb("mx", [P, NB, NQ])
        nmx = sb("nmx", [P, NB, NQ])
        rowsum = sb("rowsum", [P, NB, NQ])
        esink = sb("esink", [P, NB, NQ])
        rinv = sb("rinv", [P, NB, NQ])
        gnat = sb("gnat", [P, NB, 2 * NH])
        acol = sb("acol", [P, NB, 2, NH])
        den = sb("den", [P, NB, NH])
        hss = sb("hss", [P, NB, NH])
        layer_base = sb("layer_base", [P, 1])
        idx_u = [sb(f"idx_u{b}", [P, TOPK], U32) for b in range(NB)]
        idx_v = [sb(f"idx_v{b}", [P, TOPK], U32) for b in range(NB)]
        gate = sb("gate", [P, NB, TOPK])
        pre = sb("pre", [P, NB, TOPK])
        act_k = sb("act_k", [P, NB, TOPK])
        tops = sb("tops", [P, TOPK])
        gsum = sb("gsum", [P, 2])

        def const(name):
            a, b = CONST[name]
            return cst[:, a:b]

        ident = const("ident")

        def region(a, n):
            assert a + n <= 4 * NC * 256
            return work[:, a:a + n]

        silq = region(0, 1024).rearrange("p (h t) -> p h t", h=NH)
        kk = region(1024, 1024).rearrange("p (h t) -> p h t", h=NH)
        cum = region(2048, 1024).rearrange("p (h t) -> p h t", h=NH)
        wts = [region(3072 + 1024 * i, 1024).rearrange("p (h t) -> p h t", h=NH) for i in range(2)]
        qa_w = region(5120, 1024).rearrange("p (h t) -> p h t", h=NH)
        kk_w = region(6144, 1024).rearrange("p (h t) -> p h t", h=NH)
        hsc = region(7168, 1536).rearrange("p (h k t) -> p h k t", h=NH, k=3)
        kvraw = region(8704, 512).rearrange("p (b n) -> p b n", b=NB)
        qraw = region(9216, 2048).rearrange("p (b n) -> p b n", b=NB)
        cin = region(11264, 2048).rearrange("p (m t) -> p m t", m=2 * NH)
        cout = region(13312, 2048).rearrange("p (m t) -> p m t", m=2 * NH)
        vh = keysT[:, 8:16, :].rearrange("p a n -> p (a n)").rearrange("p (b n) -> p b n", b=NB)
        hgain = keysT[:, 0:4, :].rearrange("p a n -> p (a n)").unsqueeze(1)
        qrot = region(0, 2048).rearrange("p (b n) -> p b n", b=NB)
        krot = region(2048, 512).rearrange("p (b k d n) -> p b k d n", b=NB, k=NKV, d=2)
        rtmp = region(3072, 1024)
        rows = region(2560, 1536).rearrange("p (r t) -> p r t", r=6)
        qT = region(4096, 2048).rearrange("p (j t) -> p j t", j=NQ // 2)
        kT = region(6144, 512).rearrange("p (k t) -> p k t", k=NKV)
        probs = region(0, 1024)
        probsT = region(9216, 1024)
        gsilu = region(10240, 1024).rearrange("p (b n) -> p b n", b=NB)
        vaug = region(15360, 1024).rearrange("p (b h n) -> p b h n", b=NB, h=NH)
        mw = region(1024, 1536).rearrange("p (h t) -> p h t", h=NH)
        mp = region(2560, 1536).rearrange("p (h t) -> p h t", h=NH)
        osq = region(4096, 1024).rearrange("p (b h n) -> p b h n", b=NB, h=NH)
        om_sig = region(5120, 1024).rearrange("p (b n) -> p b n", b=NB)
        wide = [region(i * NC * 512, NC * 512) for i in range(2)]
        urow = [region(i * D, D) for i in range(RING)]
        vrow = [region((RING + i) * D, D) for i in range(RING)]
        wq = slab[1][:, 0:NC * 256].rearrange("p (c n) -> p c n", c=NC)
        keys = slab[1][:, 4096:6144].rearrange("p (a n) -> p a n", a=2 * HEADS)
        qpT = slab[1][:, 6144:6656]
        tk = slab[1][:, 6656:8192]
        topv = tk[:, 0:32].rearrange("p (s k) -> p s k", s=2)
        topi = tk[:, 32:64].bitcast(U32).rearrange("p (s k) -> p s k", s=2)
        topif = tk[:, 64:96].rearrange("p (s k) -> p s k", s=2)
        sel = tk[:, 96:112].bitcast(U32)
        selhl = tk[:, 112:144].bitcast(U32).rearrange("p (s k) -> p s k", s=2)
        selhlf = tk[:, 144:176].rearrange("p (s k) -> p s k", s=2)
        selidx = tk[:, 176:208].rearrange("p (s k) -> p s k", s=2)
        idxf = tk[:, 208:224]
        texp = tk[:, 224:240]
        left = tk[:, 240:496].rearrange("p (s n) -> p s n", s=2)
        cand = tk[:, 496:752]
        cand2 = tk[:, 752:1008]
        hot = tk[:, 1008:1520].rearrange("p (s k j) -> p s k j", s=2, k=TOPK)

        def pair(j):
            return PS[:, 2 * (j % 2):2 * (j % 2) + 2, :]

        def bank(i, n=1):
            return PS[:, i:i + n, :].rearrange("p b n -> p (b n)")

        const_loaded = signal("const_loaded", 0)
        x_loaded = signal("x_loaded", 0)
        gain_loaded = signal("gain_loaded", 2 * 16)
        gain_used = signal("gain_used", 2, start=1)
        small_loaded = signal("small_loaded", 5 * 16)
        hgain_loaded = signal("hgain_loaded", 16)
        small_used = signal("small_used", 1, start=1)
        slab_loaded = [signal("slab0_loaded", 7 * 16), signal("slab1_loaded", 6 * 16)]
        wide_loaded = [signal("wide0_loaded", 16), signal("wide1_loaded", 16)]
        wq_loaded = signal("wq_loaded", HEADS * 16)
        keys_loaded = signal("keys_loaded", 2 * HEADS * 16)
        x_ready = signal("x_ready", 2)
        sumsq_ready = signal("sumsq_ready", 2)
        var_ready = signal("var_ready", 2)
        std_ready = signal("std_ready", 2)
        normed = signal("normed", 2 * NB)
        turned = signal("turned", 3 * 8)
        turned_dve = signal("turned_dve", 3 * 4)
        turned_act = signal("turned_act", 3 * 4)
        setup_turned = signal("setup_turned", 0)
        logits_ready = signal("logits_ready", 0)
        logits_exped = signal("logits_exped", 0)
        conv_turned = signal("conv_turned", 1)
        conv_ready = signal("conv_ready", 1)
        projected = signal("projected", NS + NO, start=1)
        drained = signal("drained", NS)
        ln_args = signal("ln_args", 1)
        ln_ready = signal("ln_ready", 1)
        level_diff = signal("level_diff", NL + 1)
        level_exp = signal("level_exp", NL + 1)
        level_ops = signal("level_ops", NL + 1)
        level_scored = signal("level_scored", NL + 1)
        level_taken = signal("level_taken", NL + 1)
        gates_done = signal("gates_done", 1)
        gates_nat = signal("gates_nat", 1)
        gates_turned = signal("gates_turned", 1)
        softplus_in = signal("softplus_in", 1)
        softplus_out = signal("softplus_out", 1)
        gate_rows = signal("gate_rows", 1)
        rot_done = signal("rot_done", 1)
        qk_turned = signal("qk_turned", 3)
        qk_taken_dve = signal("qk_taken_dve", 2)
        qk_taken_act = signal("qk_taken_act", 1)
        scored = signal("scored", NBATCH)
        masked = signal("masked", NBATCH)
        exped = signal("exped", NBATCH)
        probs_turned = signal("probs_turned", NBATCH)
        probs_taken = signal("probs_taken", NBATCH)
        attended = signal("attended", NBATCH)
        attn_taken = signal("attn_taken", NBATCH)
        conved = signal("conved", 2)
        silued = signal("silued", 2)
        m_spread = signal("m_spread", 1)
        m_exp_in = signal("m_exp_in", 1)
        m_exp_out = signal("m_exp_out", 1)
        m_scored = signal("m_scored", 2)
        m_weighted = signal("m_weighted", 1)
        m_out = signal("m_out", 1)
        m_taken = signal("m_taken", 1)
        hgrn_out = signal("hgrn_out", 1)
        hgrn_sq = signal("hgrn_sq", 1)
        hgrn_var = signal("hgrn_var", 1)
        hgrn_std = signal("hgrn_std", 1)
        mixed = signal("mixed", 1)
        out_taken = signal("out_taken", NO)
        keys_turned = signal("keys_turned", 4)
        keys_taken = signal("keys_taken", 4)
        query_done = signal("query_done", HEADS, start=1)
        query_taken = signal("query_taken", HEADS)
        keyed = signal("keyed", HEADS, start=1)
        top_taken = signal("top_taken", GROUPS, start=1)
        tops_ready = signal("tops_ready", GROUPS)
        gate_exped = signal("gate_exped", GROUPS)
        idx_ready = signal("idx_ready", GROUPS)
        vidx_ready = signal("vidx_ready", GROUPS, start=1)
        u_loaded = [signal(f"u_loaded{i}", GROUPS * TOPK // RING * 16) for i in range(RING)]
        v_loaded = [signal(f"v_loaded{i}", GROUPS * TOPK // RING * 16) for i in range(RING)]
        u_free = signal("u_free", GROUPS * TOPK, start=RING)
        v_free = signal("v_free", GROUPS * TOPK, start=RING)
        dotted = signal("dotted", GROUPS)
        gelued = signal("gelued", GROUPS)
        act_ready = signal("act_ready", GROUPS)
        diag_ready = signal("diag_ready", GROUPS * TOPK)
        sum_taken = signal("sum_taken", GROUPS, start=1)
        stored = signal("stored", 0)

        waits = {e: signal(f"waits_{e}", 0) for e in ("sp", "pe", "dve", "pool")}

        block = ctx.enter_context(nc.Block())

        def stop_until(engine, name, sem, value):
            engine.wait_ge(sem, value)
            engine.sem_inc(waits[name].sem, 1)

        def layer_of(t, l):
            return t[bass.ds(l, 1)]

        @block.sync
        def _(sp):
            sp.dma_start(xs[:], x.rearrange("a (b p) d -> p (a b) d", p=P)).then_inc(x_loaded.sem, 16)
            sp.dma_start(cst[:], consts).then_inc(const_loaded.sem, 16)
            sp.dma_start(lb_rows[:], hgrn_lb_logits.rearrange("l (h p) -> (l h) p", p=P)).then_inc(const_loaded.sem, 16)

            with sp.Fori(0, DEPTH) as l:
                stop_until(sp, "sp", gain_used.sem, gain_used.upto(l, 0))
                sp.dma_start(gain[:].unsqueeze(1), layer_of(norm_mix, l).partition_broadcast(P)).then_inc(gain_loaded.sem, 16)
                stop_until(sp, "sp", projected.sem, projected.upto(l, 0))

                def load_w_in(j):
                    _, c0, n = SLABS[j]
                    sp.dma_start(slab[j % 2][:, 0:NC * n].rearrange("p (c n) -> p c n", c=NC),
                                 layer_of(w_in, l)[:, :, c0:c0 + n].rearrange("a (c p) n -> p (a c) n", p=P)
                                 ).then_inc(slab_loaded[j % 2].sem, 16)

                load_w_in(0)
                stop_until(sp, "sp", small_used.sem, small_used.upto(l, 0))
                sp.dma_start(conv_rows[:], layer_of(mlstm_conv, l).rearrange("a j (m p) -> (a j m) p", p=P)).then_inc(small_loaded.sem, 16)
                sp.dma_start(sinks[:], layer_of(attn_sinks, l).partition_broadcast(P)).then_inc(small_loaded.sem, 16)
                sp.dma_start(gate_bias[:, :, 0:NH], layer_of(mlstm_i_bias, l).partition_broadcast(P)).then_inc(small_loaded.sem, 16)
                sp.dma_start(gate_bias[:, :, NH:2 * NH], layer_of(mlstm_f_bias, l).partition_broadcast(P)).then_inc(small_loaded.sem, 16)
                sp.dma_start(gates_w[:], layer_of(w_in, l)[:, :, COLS["gates"]:COLS["gates"] + 2 * NH]
                             .rearrange("a (c p) n -> p (a c) n", p=P)).then_inc(small_loaded.sem, 16)
                stop_until(sp, "sp", query_done.sem, query_done.upto(l, 0))
                stop_until(sp, "sp", vidx_ready.sem, vidx_ready.upto(l, 0))
                load_w_in(1)
                sp.dma_start(hgain, layer_of(hgrn_out_norm, l).partition_broadcast(P)).then_inc(hgain_loaded.sem, 16)
                for j in range(2, NS):
                    stop_until(sp, "sp", projected.sem, projected.upto(l, j - 1))
                    load_w_in(j)

                def load_w_out(o, dst, s):
                    sp.dma_start(dst.rearrange("p (c n) -> p c n", c=NC),
                                 layer_of(w_out, l)[:, :, o * 512:(o + 1) * 512].rearrange("a (c p) n -> p (a c) n", p=P)
                                 ).then_inc(s.sem, 16)

                stop_until(sp, "sp", projected.sem, projected.upto(l, NS - 1))
                load_w_out(0, slab[1][:], slab_loaded[1])
                stop_until(sp, "sp", gain_used.sem, gain_used.upto(l, 1))
                sp.dma_start(gain[:].unsqueeze(1), layer_of(norm_ffn, l).partition_broadcast(P)).then_inc(gain_loaded.sem, 16)
                stop_until(sp, "sp", projected.sem, projected.upto(l, NS))
                load_w_out(1, slab[0][:], slab_loaded[0])
                stop_until(sp, "sp", mixed.sem, mixed.upto(l, 1))
                load_w_out(2, wide[0], wide_loaded[0])
                load_w_out(3, wide[1], wide_loaded[1])
                stop_until(sp, "sp", projected.sem, projected.upto(l, NS + 1))
                for s in range(2):
                    for h in range(HEADS):
                        sp.dma_start(keys[:, s * HEADS + h, :], layer_of(peer_sub_keys, l)[:, s, h].rearrange("a n d -> (a n) d")
                                     ).then_inc(keys_loaded.sem, 16)

                with sp.Fori(0, HEADS) as h:
                    stop_until(sp, "sp", query_done.sem, query_done.upto(l, h))
                    sp.dma_start(wq, layer_of(peer_query, l)[:, :, bass.ds(h * 256, 256)]
                                 .rearrange("a (c p) n -> p (a c) n", p=P)).then_inc(wq_loaded.sem, 16)

            stop_until(sp, "sp", gain_used.sem, gain_used.upto(DEPTH, 0))
            sp.dma_start(gain[:], norm_final.partition_broadcast(P)).then_inc(gain_loaded.sem, 16)
            for b in range(NB):
                sp.wait_ge(normed.sem, normed.upto(DEPTH, b + 1))
                sp.dma_start(out[0, b * P:(b + 1) * P, :], hn[:, b, :]).then_inc(stored.sem, 16)
            sp.wait_ge(stored.sem, 16 * NB)

        @block.tensor
        def _(pe):
            for s in (projected, query_done, keyed):
                pe.sem_inc(s.sem, s.start)
            pe.wait_ge(const_loaded.sem, 32)
            pe.transpose(PS[:, 7, 0:DEPTH * NH], lb_rows[:], ident[0:DEPTH * NH, 0:DEPTH * NH]).then_inc(setup_turned.sem, 1)

            def turn(l, use, src):
                for f in range(8):
                    if f >= 4:
                        s, n = (turned_act, f // 2 - 1) if f % 2 else (turned_dve, f // 2 - 1)
                        pe.wait_ge(s.sem, s.upto(l, 4 * use + n))
                    for i in range(4):
                        c, b = 2 * f + i // 2, i % 2
                        t = pe.transpose(PS[:, 4 + f % 4, i * P:(i + 1) * P], src[:, b, c * P:(c + 1) * P], ident)
                    t.then_inc(turned.sem, 1)
                pe.wait_ge(turned_dve.sem, turned_dve.upto(l, 4 * use + 4))
                pe.wait_ge(turned_act.sem, turned_act.upto(l, 4 * use + 4))

            def natural(dst, w, n, hooks):
                for c in range(NC):
                    for b in range(NB):
                        mm = pe.matmul(dst[:, b, 0:n], hT[:, c, b * P:(b + 1) * P], w[:, c, :],
                                       start=(c == 0), stop=(c == NC - 1))
                    if c % 4 == 3 and c < NC - 1:
                        hooks[c // 4]()
                return mm

            def transposed(dst, w, hooks):
                d = dst.rearrange("p b (m t) -> p (b m) t", m=2)
                for m in range(4):
                    for c in range(NC):
                        mm = pe.matmul(d[:, m, :], w[:, c, m * P:(m + 1) * P], hT[:, c, :],
                                       start=(c == 0), stop=(c == NC - 1))
                    if m < 3:
                        hooks[m]()
                return mm

            with pe.Fori(0, DEPTH) as l:
                def nothing():
                    pass

                def conv_weights():
                    stop_until(pe, "pe", small_loaded.sem, small_loaded.upto(l, 5 * 16))
                    pe.transpose(PS[:, 7, 0:CONV * 2 * NH], conv_rows[:], ident[0:CONV * 2 * NH, 0:CONV * 2 * NH]).then_inc(conv_turned.sem, 1)

                def level(i):
                    if i > 0:
                        pe.wait_ge(level_taken.sem, level_taken.upto(l, i))
                    d = bank(4, 2).rearrange("p (h t) -> p h t", h=NH)
                    if i < NL:
                        pe.wait_ge(level_ops.sem, level_ops.upto(l, i + 1))
                    q, k = (qa_w, kk_w) if i < NL else (silq, kk)
                    for h in range(NH):
                        for b in range(NB):
                            r = slice(b * P, (b + 1) * P)
                            mm = pe.matmul(d[:, h, r], k[:, h, r], q[:, h, r], start=True, stop=True)
                    if i == NL:
                        pe.wait_ge(level_ops.sem, level_ops.upto(l, NL + 1))
                        for h in range(NH):
                            mm = pe.matmul(PS[:, 6, h * P:(h + 1) * P], kk_w[:, h, 0:P], qa_w[:, h, P:SEQ], start=True, stop=True)
                    mm.then_inc(level_scored.sem, 1)

                def gates():
                    pe.wait_ge(conv_ready.sem, conv_ready.upto(l, 1))
                    for b in range(NB):
                        for c in range(NC):
                            mm = pe.matmul(PS[:, 7, b * 8:b * 8 + 8], hT[:, c, b * P:(b + 1) * P], gates_w[:, c, :],
                                           start=(c == 0), stop=(c == NC - 1))
                    mm.then_inc(gates_done.sem, 1)

                def gate_turn():
                    pe.wait_ge(gates_nat.sem, gates_nat.upto(l, 1))
                    for k in range(2):
                        for b in range(NB):
                            mm = pe.transpose(PS[0:NH, 7, k * SEQ + b * P:k * SEQ + (b + 1) * P], gnat[:, b, k * NH:(k + 1) * NH], ident)
                    mm.then_inc(gates_turned.sem, 1)

                def turn_q():
                    pe.wait_ge(rot_done.sem, rot_done.upto(l, 1))
                    pe.wait_ge(level_taken.sem, level_taken.upto(l, NL + 1))
                    pe.wait_ge(gate_rows.sem, gate_rows.upto(l, 1))
                    d = bank(4, 4).rearrange("p (j t) -> p j t", j=NQ // 2)
                    for j in range(NQ // 2):
                        for b in range(NB):
                            mm = pe.transpose(d[:, j, b * P:(b + 1) * P], qrot[:, b, j * P:(j + 1) * P], ident)
                        if j % 4 == 3:
                            mm.then_inc(qk_turned.sem, 1)

                def turn_k():
                    pe.wait_ge(qk_taken_dve.sem, qk_taken_dve.upto(l, 1))
                    for k in range(NKV):
                        for b in range(NB):
                            mm = pe.transpose(PS[:, 4, (2 * k + b) * P:(2 * k + b + 1) * P],
                                              krot[:, b, k].rearrange("p d n -> p (d n)"), ident)
                    mm.then_inc(qk_turned.sem, 1)

                def scores(n):
                    b, h0, nh = BATCHES[n]
                    if n == 0:
                        pe.wait_ge(qk_taken_dve.sem, qk_taken_dve.upto(l, 2))
                        pe.wait_ge(qk_taken_act.sem, qk_taken_act.upto(l, 1))
                    else:
                        pe.wait_ge(masked.sem, masked.upto(l, n))
                    keys_n = (b + 1) * P
                    d = PS[:, 6:8, :].rearrange("p r (j s) -> p r j s", j=nh // 2)
                    for i in range(nh):
                        h = h0 + i
                        r = slice(DH * (h % 2), DH * (h % 2) + DH)
                        mm = pe.matmul(d[:, i % 2, i // 2, :], qT[r, h // 2, b * P:(b + 1) * P], kT[r, h // (NQ // NKV), 0:keys_n],
                                       start=True, stop=True)
                    mm.then_inc(scored.sem, 1)

                def turn_probs(n):
                    b, h0, nh = BATCHES[n]
                    pe.wait_ge(exped.sem, exped.upto(l, n + 1))
                    if n > 0:
                        pe.wait_ge(attn_taken.sem, attn_taken.upto(l, n))
                    d = bank(4, 2).rearrange("p (k t) -> p k t", k=8)
                    pr = probs.rearrange("p (k s) -> p k s", k=8)
                    for k in range(8):
                        mm = pe.transpose(d[:, k, :], pr[:, k, :], ident)
                    mm.then_inc(probs_turned.sem, 1)

                def attend(n):
                    b, h0, nh = BATCHES[n]
                    pe.wait_ge(probs_taken.sem, probs_taken.upto(l, n + 1))
                    pt = probsT.rearrange("p (k t) -> p k t", k=8)
                    for i in range(nh):
                        kv = (h0 + i) // (NQ // NKV)
                        for kb in range(b + 1):
                            mm = pe.matmul(PS[:, 4, i * DH:(i + 1) * DH], pt[:, i * (b + 1) + kb, :],
                                           kvraw[:, kb, P + kv * DH:P + (kv + 1) * DH], start=(kb == 0), stop=(kb == b))
                    mm.then_inc(attended.sem, 1)

                def spread_m():
                    pe.wait_ge(attn_taken.sem, attn_taken.upto(l, NBATCH))
                    a, _ = CONST["pick"]
                    d = bank(4, 2).rearrange("p (h t) -> p h t", h=NH)
                    for h in range(NH):
                        pe.matmul(d[:, h, :], cst[0:NH, a + h * P:a + (h + 1) * P], rows[0:NH, 3, :], start=True, stop=True)
                    for b in range(NB):
                        for k, r in ((0, 2), (1, 4)):
                            mm = pe.transpose(PS[:, 6, (2 * b + k) * NH:(2 * b + k + 1) * NH],
                                              rows[0:NH, r, b * P:(b + 1) * P], ident[0:NH, 0:NH])
                    mm.then_inc(m_spread.sem, 1)

                def m_scores(i):
                    pe.wait_ge(silued.sem, silued.upto(l, 2))
                    pe.wait_ge(m_exp_in.sem, m_exp_in.upto(l, 1))
                    base = 6 if i == 0 else 4
                    for j in range(2):
                        h = 2 * i + j
                        pe.matmul(PS[:, base + j, 0:SEQ], cout[:, NH + h, 0:P], cout[:, h, :], start=True, stop=True)
                        mm = pe.matmul(PS[:, base + j, SEQ:SEQ + P], cout[:, NH + h, P:SEQ], cout[:, h, P:SEQ], start=True, stop=True)
                    mm.then_inc(m_scored.sem, 1)

                def m_attend():
                    pe.wait_ge(m_weighted.sem, m_weighted.upto(l, 1))
                    pe.wait_ge(drained.sem, drained.upto(l, 9))
                    for b in range(NB):
                        for h in range(NH):
                            for kb in range(b + 1):
                                w = mp[:, h, b * P:(b + 1) * P] if kb == 0 else mp[:, h, SEQ:SEQ + P]
                                pe.matmul(PS[:, 4 + b, h * P:(h + 1) * P], w, vaug[:, kb, h, :], start=(kb == 0), stop=(kb == b))
                    for b in range(NB):
                        for h in range(NH):
                            for kb in range(b + 1):
                                w = mp[:, h, b * P:(b + 1) * P] if kb == 0 else mp[:, h, SEQ:SEQ + P]
                                mm = pe.matmul(PS[:, 6, b * NH + h:b * NH + h + 1], w, ones[:, 0:1], start=(kb == 0), stop=(kb == b))
                    mm.then_inc(m_out.sem, 1)

                def hgrn_attend():
                    pe.wait_ge(m_taken.sem, m_taken.upto(l, 1))
                    for b in range(NB):
                        for h in range(NH):
                            mm = pe.matmul(PS[:, 4 + b, h * P:(h + 1) * P], hsc[:, h, 2 * b, :], vh[:, 0, h * P:(h + 1) * P],
                                           start=True, stop=(b == 0))
                            if b == 1:
                                mm = pe.matmul(PS[:, 4 + b, h * P:(h + 1) * P], hsc[:, h, 1, :], vh[:, 1, h * P:(h + 1) * P],
                                               start=False, stop=True)
                    mm.then_inc(hgrn_out.sem, 1)

                def batch_step(n):
                    def go():
                        if n > 0:
                            attend(n - 1)
                        if n < NBATCH:
                            scores(n)
                    return go

                steps = {}
                steps[0] = conv_weights
                for i in range(NL + 1):
                    steps[8 + i] = lambda i=i: level(i)
                steps[16] = gates
                steps[18] = gate_turn
                steps[21], steps[22] = turn_q, turn_k
                for n in range(NBATCH + 1):
                    steps[23 + 2 * n] = batch_step(n)
                    if n < NBATCH:
                        steps[24 + 2 * n] = lambda n=n: turn_probs(n)
                steps[36] = spread_m
                steps[37] = lambda: m_scores(0)
                steps[38] = lambda: m_scores(1)
                steps[40] = m_attend
                steps[41] = hgrn_attend

                for b in range(NB):
                    pe.wait_ge(normed.sem, normed.upto(l, b + 1))
                turn(l, 0, hn)
                for j in range(NS):
                    name, _, n = SLABS[j]
                    i, k = j % 2, j // 2 + 1
                    pe.wait_ge(slab_loaded[i].sem, slab_loaded[i].upto(l, 16 * k))
                    if j >= 2:
                        pe.wait_ge(drained.sem, drained.upto(l, j - 1))
                    w = slab[i][:, 0:NC * n].rearrange("p (c n) -> p c n", c=NC)
                    hooks = [steps.get(4 * j + q, nothing) for q in range(4)]
                    mm = (transposed(pair(j), w, hooks) if name in ("fh", "qh", "qkm0", "qkm1")
                          else natural(pair(j), w, n, hooks))
                    mm.then_inc(projected.sem, 1)
                    hooks[3]()

                pe.wait_ge(mixed.sem, mixed.upto(l, 1))
                turn(l, 1, hn)
                for o in range(NO):
                    if o < 2:
                        i, k = 1 - o, (6, 7)[o]
                        pe.wait_ge(slab_loaded[i].sem, slab_loaded[i].upto(l, 16 * k))
                        w = slab[i][:]
                        pe.wait_ge(drained.sem, drained.upto(l, NS))
                    else:
                        pe.wait_ge(wide_loaded[o - 2].sem, wide_loaded[o - 2].upto(l, 16))
                        w = wide[o - 2]
                        pe.wait_ge(out_taken.sem, out_taken.upto(l, o - 1))
                    natural(pair(o), w.rearrange("p (c n) -> p c n", c=NC), 512, [nothing] * 4).then_inc(projected.sem, 1)

                pe.wait_ge(keys_loaded.sem, keys_loaded.upto(l, 2 * HEADS * 16))
                for f in range(4):
                    for i in range(4):
                        mm = pe.transpose(PS[:, 4 + f, i * P:(i + 1) * P], keys[:, 4 * f + i, :], ident)
                    mm.then_inc(keys_turned.sem, 1)
                for b in range(NB):
                    pe.wait_ge(normed.sem, normed.upto(l, NB + b + 1))
                pe.wait_ge(keys_taken.sem, keys_taken.upto(l, 4))
                turn(l, 2, hn)

                def query(h):
                    pe.wait_ge(wq_loaded.sem, (l * HEADS + h) * 16 + 16)
                    for s in range(2):
                        for c in range(NC):
                            mm = pe.matmul(PS[:, 4, s * SEQ:(s + 1) * SEQ], wq[:, c, s * P:(s + 1) * P], hT[:, c, :],
                                           start=(c == 0), stop=(c == NC - 1))
                    mm.then_inc(query_done.sem, 1)

                def key_scores(h):
                    pe.wait_ge(query_taken.sem, l * HEADS + h + 1)
                    pe.wait_ge(top_taken.sem, top_taken.upto(l, h * NB))
                    for b in range(NB):
                        for s in range(2):
                            mm = pe.matmul(PS[:, 5, (2 * b + s) * P:(2 * b + s + 1) * P],
                                           qpT[:, s * SEQ + b * P:s * SEQ + (b + 1) * P],
                                           keysT[:, bass.ds(s * HEADS + h, 1), :], start=True, stop=True)
                    mm.then_inc(keyed.sem, 1)

                def sum_rows(h, b, k):
                    g = h * NB + b
                    slot = (l * GROUPS + g) * TOPK + k
                    if k == 0:
                        pe.wait_ge(sum_taken.sem, sum_taken.upto(l, g))
                    pe.wait_ge(diag_ready.sem, slot + 1)
                    pe.wait_ge(v_loaded[k % RING].sem, ((l * GROUPS + g) * (TOPK // RING) + k // RING) * 16 + 16)
                    for j in range(4):
                        mm = pe.matmul(PS[:, j, :], diag[:, k % RING, :], vrow[k % RING][:, j * 512:(j + 1) * 512],
                                       start=(k == 0), stop=(k == TOPK - 1))
                    mm.then_inc(v_free.sem, 1)

                query(0)
                key_scores(0)
                with pe.Fori(0, HEADS - 1) as h:
                    query(h + 1)
                    for k in range(TOPK):
                        sum_rows(h, 0, k)
                        if k == 1:
                            key_scores(h + 1)
                    for k in range(TOPK):
                        sum_rows(h, 1, k)
                for b in range(NB):
                    for k in range(TOPK):
                        sum_rows(HEADS - 1, b, k)

        @block.scalar
        def _(act):
            def sumsq(l, use):
                act.wait_ge(x_ready.sem, x_ready.upto(l, use + 1))
                for b in range(NB):
                    a = act.activation(hn[:, b, :], xs[:, b, :], ACT.Square, accum_out=ss[:, b:b + 1])
                a.then_inc(sumsq_ready.sem, 1)
                act.wait_ge(var_ready.sem, var_ready.upto(l, use + 1))
                act.activation(rms[:], ss[:], ACT.Sqrt).then_inc(std_ready.sem, 1)

            def take_turned(l, use):
                for f in range(1, 8, 2):
                    act.wait_ge(turned.sem, turned.upto(l, 8 * use + f + 1))
                    act.activation(hT[:, 2 * f:2 * f + 2, :].rearrange("p c t -> p (c t)"), bank(4 + f % 4), ACT.Copy
                                   ).then_inc(turned_act.sem, 1)

            act.wait_ge(logits_ready.sem, 1)
            act.activation(lb_all[:, 0].rearrange("p l h -> p (l h)"), lb_all[:, 0].rearrange("p l h -> p (l h)"), ACT.Exp
                           ).then_inc(logits_exped.sem, 1)

            with act.Fori(0, DEPTH) as l:
                def drain(j):
                    act.wait_ge(projected.sem, projected.upto(l, j + 1))
                    name = SLABS[j][0]
                    p = pair(j)
                    pt = p.rearrange("p b (m t) -> p (b m) t", m=2)
                    if name == "fh":
                        act.activation(cum, pt, ACT.Sigmoid)
                        a = act.activation(kk, pt, ACT.Sigmoid, scale=-1.0)
                    elif name == "qh":
                        a = act.activation(silq, pt, ACT.Silu)
                    elif name in ("qa0", "qa1"):
                        c = 512 * int(name[2])
                        a = act.activation(qraw[:, :, c:c + 512], p, ACT.Copy)
                    elif name == "kv":
                        a = act.activation(kvraw, p[:, :, 0:256], ACT.Copy)
                    elif name in ("qkm0", "qkm1"):
                        m = 4 * int(name[3])
                        a = act.activation(cin[:, m:m + 4, :], pt, ACT.Copy)
                    elif name == "ih":
                        a = act.activation(vh, p, ACT.Copy)
                    elif name == "vm":
                        a = act.activation(vaug.rearrange("p b h n -> p b (h n)"), p, ACT.Copy)
                    elif name == "gh":
                        a = act.activation(gsilu, p, ACT.Silu)
                    else:
                        a = act.activation(om_sig, p, ACT.Sigmoid)
                    a.then_inc(drained.sem, 1)

                def level_exps(i):
                    act.wait_ge(level_diff.sem, level_diff.upto(l, i + 1))
                    w = wts[i % 2]
                    if i < NL:
                        act.activation(w, w, ACT.Abs)
                        act.drain()
                        a = act.activation(w, w, ACT.Exp, scale=-1.0)
                    else:
                        act.activation(w[:, :, 0:P], w[:, :, 0:P], ACT.Exp)
                        a = act.activation(w[:, :, P:SEQ], cum[:, :, P:SEQ], ACT.Exp)
                    a.then_inc(level_exp.sem, 1)

                def batch_exps(n):
                    b, h0, nh = BATCHES[n]
                    act.wait_ge(masked.sem, masked.upto(l, n + 1))
                    pr = probs.rearrange("p (h s) -> p h s", h=nh)
                    act.activation(esink[:, b, h0:h0 + nh], esink[:, b, h0:h0 + nh], ACT.Exp)
                    for i in range(nh):
                        h = h0 + i
                        a = act.activation(pr[:, i, :], pr[:, i, :], ACT.Exp, bias=nmx[:, b, h:h + 1], scale=DH ** -0.5,
                                           accum_out=rowsum[:, b, h:h + 1])
                    a.then_inc(exped.sem, 1)

                def silu_conv(i):
                    act.wait_ge(conved.sem, conved.upto(l, i + 1))
                    act.activation(cout[:, 4 * i:4 * i + 4, :], cout[:, 4 * i:4 * i + 4, :], ACT.Silu).then_inc(silued.sem, 1)

                sumsq(l, 0)
                take_turned(l, 0)
                drain(0)
                act.wait_ge(ln_args.sem, ln_args.upto(l, 1))
                act.activation(cum, cum, ACT.Ln)
                act.activation(wts[0], wts[0], ACT.Ln, scale=1.0 / FLOOR).then_inc(ln_ready.sem, 1)
                drain(1)
                for i in range(5):
                    level_exps(i)
                drain(2)
                for i in range(5, NL + 1):
                    level_exps(i)
                drain(3)
                drain(4)
                act.wait_ge(softplus_in.sem, softplus_in.upto(l, 1))
                act.activation(rows[0:NH, 5, :], rows[0:NH, 1, :], ACT.Abs)
                act.drain()
                act.activation(rows[0:NH, 5, :], rows[0:NH, 5, :], ACT.Exp, scale=-1.0)
                act.drain()
                act.activation(rows[0:NH, 5, :], rows[0:NH, 5, :], ACT.Ln, bias=1.0).then_inc(softplus_out.sem, 1)
                act.wait_ge(qk_turned.sem, qk_turned.upto(l, 3))
                act.activation(kT.rearrange("p k t -> p (k t)"), bank(4), ACT.Copy).then_inc(qk_taken_act.sem, 1)
                batch_exps(0)
                drain(5)
                batch_exps(1)
                silu_conv(0)
                batch_exps(2)
                batch_exps(3)
                drain(6)
                batch_exps(4)
                silu_conv(1)
                drain(7)
                batch_exps(5)
                act.wait_ge(m_exp_in.sem, m_exp_in.upto(l, 1))
                act.activation(mw, mw, ACT.Exp, scale=-1.0)
                act.activation(acol[:, :, 1, :], acol[:, :, 1, :], ACT.Exp).then_inc(m_exp_out.sem, 1)
                drain(8)
                drain(9)
                act.wait_ge(hgrn_out.sem, hgrn_out.upto(l, 1))
                act.activation(osq.rearrange("p b h n -> p (b h n)"), bank(4, 2), ACT.Square).then_inc(hgrn_sq.sem, 1)
                act.wait_ge(hgrn_var.sem, hgrn_var.upto(l, 1))
                act.activation(hss[:], hss[:], ACT.Sqrt).then_inc(hgrn_std.sem, 1)
                drain(10)
                take_turned(l, 1)
                sumsq(l, 1)
                for f in range(4):
                    act.wait_ge(keys_turned.sem, keys_turned.upto(l, f + 1))
                    act.activation(keysT[:, 4 * f:4 * f + 4, :].rearrange("p a n -> p (a n)"), bank(4 + f), ACT.Copy
                                   ).then_inc(keys_taken.sem, 1)
                take_turned(l, 2)

                def take_query(h):
                    act.wait_ge(query_done.sem, query_done.upto(l, h + 1))
                    act.wait_ge(keyed.sem, keyed.upto(l, h))
                    act.activation(qpT, bank(4), ACT.Copy).then_inc(query_taken.sem, 1)

                def gate_exp(h, b):
                    act.wait_ge(tops_ready.sem, l * GROUPS + h * NB + b + 1)
                    act.activation(texp, tops[:], ACT.Exp, bias=gsum[:, 0:1], accum_out=gsum[:, 1:2]).then_inc(gate_exped.sem, 1)

                def gelu(h, b):
                    act.wait_ge(dotted.sem, l * GROUPS + h * NB + b + 1)
                    act.activation(act_k[:, b, :], pre[:, b, :], ACT.Gelu).then_inc(gelued.sem, 1)

                def diagonals(h, b, ks):
                    g = h * NB + b
                    if ks[0] == 0:
                        act.wait_ge(act_ready.sem, l * GROUPS + g + 1)
                    for k in ks:
                        act.wait_ge(v_free.sem, (l * GROUPS + g) * TOPK + k + 1)
                        act.activation(diag[:, k % RING, :], ident, ACT.Copy, scale=act_k[:, b, k:k + 1]).then_inc(diag_ready.sem, 1)

                take_query(0)
                gate_exp(0, 0)
                gate_exp(0, 1)
                gelu(0, 0)
                with act.Fori(0, HEADS - 1) as h:
                    diagonals(h, 0, range(0, 2))
                    take_query(h + 1)
                    diagonals(h, 0, range(2, 10))
                    gate_exp(h + 1, 0)
                    diagonals(h, 0, range(10, TOPK))
                    gelu(h, 1)
                    diagonals(h, 1, range(0, 8))
                    gate_exp(h + 1, 1)
                    diagonals(h, 1, range(8, TOPK))
                    gelu(h + 1, 0)
                diagonals(HEADS - 1, 0, range(TOPK))
                gelu(HEADS - 1, 1)
                diagonals(HEADS - 1, 1, range(TOPK))

            sumsq(DEPTH, 0)

        @block.gpsimd
        def _(pool):
            tables = {"u": peer_u.rearrange("l e d -> (l e) d"), "v": peer_v.rearrange("l e d -> (l e) d")}

            with pool.Fori(0, DEPTH) as l:
                def fetch(kind, h, b, k):
                    g = h * NB + b
                    idx, free, rows_, loaded = ((idx_u, u_free, urow, u_loaded) if kind == "u"
                                                else (idx_v, v_free, vrow, v_loaded))
                    ready = idx_ready if kind == "u" else vidx_ready
                    if k == 0:
                        pool.wait_ge(ready.sem, ready.upto(l, g + 1))
                    stop_until(pool, "pool", free.sem, (l * GROUPS + g) * TOPK + k + 1)
                    pool.indirect_dma_start(out=rows_[k % RING], out_offset=None, in_=tables[kind],
                                            in_offset=bass.IndirectOffsetOnAxis(ap=idx[b][:, k:k + 1], axis=0)
                                            ).then_inc(loaded[k % RING].sem, 16)

                for k in range(TOPK):
                    fetch("u", 0, 0, k)
                with pool.Fori(0, HEADS - 1) as h:
                    for k in range(TOPK):
                        fetch("u", h, 1, k)
                        fetch("v", h, 0, k)
                    for k in range(TOPK):
                        fetch("u", h + 1, 0, k)
                        fetch("v", h, 1, k)
                for k in range(TOPK):
                    fetch("u", HEADS - 1, 1, k)
                    fetch("v", HEADS - 1, 0, k)
                for k in range(TOPK):
                    fetch("v", HEADS - 1, 1, k)

        @block.vector
        def _(dve):
            def bc(ap, shape):
                return ap.to_broadcast(shape)

            for s in (u_free, v_free, gain_used, small_used, top_taken, vidx_ready, sum_taken):
                dve.sem_inc(s.sem, s.start)
            dve.memset(ones[:], 1.0)
            dve.memset(layer_base[:], 0.0)
            dve.wait_ge(x_loaded.sem, 16)
            dve.wait_ge(const_loaded.sem, 32)
            dve.drain()
            dve.wait_ge(setup_turned.sem, 1)
            z = lb_all[:, 0]
            dve.tensor_copy(z.rearrange("p l h -> p (l h)"), PS[:, 7, 0:DEPTH * NH])
            dve.drain()
            dve.tensor_tensor(lbt[:, 0, :], z[:, 0, :], z[:, 1, :], ALU.max)
            dve.drain()
            for i in range(DEPTH):
                dve.tensor_tensor(z[:, i, :], z[:, i, :], lbt[:, 0, :], ALU.subtract)
            dve.drain().then_inc(logits_ready.sem, 1)
            dve.wait_ge(logits_exped.sem, 1)
            dve.tensor_tensor(lbt[:, 0, :], z[:, 0, :], z[:, 1, :], ALU.add)
            dve.drain()
            dve.reciprocal(lbt[:, 1, :], lbt[:, 0, :])
            dve.drain()
            for i in range(DEPTH):
                dve.tensor_tensor(lbt[:, 2 + i, :], z[:, i, :], lbt[:, 1, :], ALU.mult)
            dve.drain()
            dve.tensor_tensor(lbt[:, 0, :], lbt[:, 2, :], lbt[:, 3, :], ALU.add)
            dve.drain()
            dve.tensor_tensor(z[:, 0, :], lbt[:, 2, :], lbt[:, 2, :], ALU.subtract)
            dve.tensor_tensor(z[:, 1, :], lbt[:, 0, :], lbt[:, 2, :], ALU.subtract)
            dve.drain()
            dve.tensor_scalar(lb_all[:, 1], z, -1.0, 1.0, ALU.mult, ALU.add)
            dve.drain().then_inc(x_ready.sem, 1)

            def normalise(l, use):
                dve.wait_ge(sumsq_ready.sem, sumsq_ready.upto(l, use + 1))
                dve.tensor_scalar(ss[:], ss[:], 1.0 / D, EPS, ALU.mult, ALU.add).then_inc(var_ready.sem, 1)
                dve.wait_ge(std_ready.sem, std_ready.upto(l, use + 1))
                dve.reciprocal(rstd[:], rms[:])
                dve.drain()
                dve.wait_ge(gain_loaded.sem, gain_loaded.upto(l, 16 * (use + 1)))
                for b in range(NB):
                    dve.scalar_tensor_tensor(out=hn[:, b, :], in0=xs[:, b, :], scalar=rstd[:, b:b + 1], in1=gain[:],
                                             op0=ALU.mult, op1=ALU.mult).then_inc(normed.sem, 1)
                dve.drain().then_inc(gain_used.sem, 1)

            def take_turned(l, use):
                for f in range(0, 8, 2):
                    dve.wait_ge(turned.sem, turned.upto(l, 8 * use + f + 1))
                    dve.tensor_copy(hT[:, 2 * f:2 * f + 2, :].rearrange("p c t -> p (c t)"), bank(4 + f % 4)
                                    ).then_inc(turned_dve.sem, 1)

            with dve.Fori(0, DEPTH) as l:
                normalise(l, 0)
                take_turned(l, 0)

                dve.wait_ge(small_loaded.sem, small_loaded.upto(l, 5 * 16))
                dve.tensor_scalar(sinks8[:], sinks[:, 0, :], DH ** 0.5, None, ALU.mult)
                dve.tensor_copy(lb[:], lb_all[:, :, bass.ds(l, 1), :].rearrange("p k a h -> p k (a h)"))
                dve.memset(hsc, 0.0)
                dve.wait_ge(conv_turned.sem, conv_turned.upto(l, 1))
                dve.tensor_copy(conv_w[:].rearrange("p j m -> p (j m)"), PS[:, 7, 0:CONV * 2 * NH]).then_inc(conv_ready.sem, 1)

                dve.drain()
                dve.wait_ge(drained.sem, drained.upto(l, 1))
                dve.tensor_tensor(kk, kk, bc(lb[:, 1, :].unsqueeze(2), [P, NH, SEQ]), ALU.mult)
                for h in range(NH):
                    dve.tensor_scalar(cum[:, h, :], cum[:, h, :], lb[:, 1, h:h + 1], lb[:, 0, h:h + 1], ALU.mult, ALU.add)
                dve.drain()
                dve.tensor_scalar(wts[0], cum, FLOOR, TINY, ALU.min, ALU.max)
                dve.drain()
                dve.tensor_scalar(cum, cum, FLOOR, None, ALU.max)
                dve.drain().then_inc(ln_args.sem, 1)
                dve.wait_ge(ln_ready.sem, ln_ready.upto(l, 1))
                dve.tensor_tensor(cum, cum, wts[0], ALU.add)
                dve.drain()
                for h in range(NH):
                    for b in range(NB):
                        r = cum[:, h, b * P:(b + 1) * P]
                        dve.tensor_tensor_scan(r, ones[:], r, 0.0, ALU.mult, ALU.add)
                dve.drain()

                def difference(i):
                    w = wts[i % 2]
                    if i < NL:
                        L = LEVELS[i]
                        n = NH * SEQ // (2 * L)
                        c = cum.rearrange("p h t -> p (h t)").rearrange("p (g u) -> p g u", u=2 * L)
                        o = w.rearrange("p h t -> p (h t)").rearrange("p (g u) -> p g u", u=2 * L)
                        d = dve.tensor_tensor(o, c, bc(c[:, :, L - 1:L], [P, n, 2 * L]), ALU.subtract)
                    else:
                        d = dve.tensor_tensor(w[:, :, 0:P], bc(cum[:, :, P - 1:P], [P, NH, P]), cum[:, :, 0:P], ALU.subtract)
                    d.then_inc(level_diff.sem, 1)

                def weigh(i):
                    dve.wait_ge(level_exp.sem, level_exp.upto(l, i + 1))
                    if i == 0:
                        dve.wait_ge(drained.sem, drained.upto(l, 2))
                    else:
                        dve.wait_ge(level_scored.sem, level_scored.upto(l, min(i, NL)))
                    w = wts[i % 2]
                    tq, tk_ = (slice(0, SEQ), slice(0, SEQ)) if i < NL else (slice(P, SEQ), slice(0, P))
                    dve.tensor_tensor(qa_w[:, :, tq], silq[:, :, tq], w[:, :, tq], ALU.mult)
                    dve.tensor_tensor(kk_w[:, :, tk_], kk[:, :, tk_], w[:, :, tk_], ALU.mult).then_inc(level_ops.sem, 1)

                def take_level(i):
                    stop_until(dve, "dve", level_scored.sem, level_scored.upto(l, i + 1))
                    a, _ = CONST["levels"]
                    m = cst[:, a + i * P:a + (i + 1) * P] if i < NL else ident
                    m = m.bitcast(I32).unsqueeze(1).unsqueeze(1).to_broadcast([P, NH, NB, P])
                    d = bank(4, 2).rearrange("p (h b t) -> p h b t", h=NH, b=NB)
                    c = dve.copy_predicated(hsc[:, :, 0:2, :], m, d)
                    if i == NL:
                        c = dve.tensor_copy(hsc[:, :, 2, :], PS[:, 6, :].rearrange("p (h t) -> p h t", h=NH))
                    dve.drain().then_inc(level_taken.sem, 1)

                difference(0)
                for i in range(NL + 1):
                    weigh(i)
                    if i < NL:
                        difference(i + 1)
                        take_level(i)
                take_level(NL)

                dve.wait_ge(gates_done.sem, gates_done.upto(l, 1))
                dve.tensor_tensor(gnat[:], PS[:, 7, 0:16].rearrange("p (b k) -> p b k", b=NB), bc(gate_bias[:], [P, NB, 2 * NH]),
                                  ALU.add).then_inc(gates_nat.sem, 1)

                cs = [const(n).rearrange("p (b f) -> p b f", b=NB).unsqueeze(2) for n in ("cos", "sin")]

                def rotate(x1, x2, r1, r2, n, tmp):
                    cos, sin = (bc(c, [P, NB, n, 32]) for c in cs)
                    dve.tensor_tensor(r1, x1, cos, ALU.mult)
                    dve.tensor_tensor(tmp, x2, sin, ALU.mult)
                    dve.tensor_tensor(r2, x2, cos, ALU.mult)
                    dve.drain()
                    dve.tensor_tensor(r1, r1, tmp, ALU.subtract)
                    dve.drain()
                    dve.tensor_tensor(tmp, x1, sin, ALU.mult)
                    dve.drain()
                    dve.tensor_tensor(r2, r2, tmp, ALU.add)
                    dve.drain()

                dve.wait_ge(drained.sem, drained.upto(l, 4))
                q5 = qraw.rearrange("p b (h w f) -> p b h w f", h=NQ, w=2)
                r5 = qrot.rearrange("p b (h w f) -> p b h w f", h=NQ, w=2)
                rotate(q5[:, :, :, 0, :], q5[:, :, :, 1, :], r5[:, :, :, 0, :], r5[:, :, :, 1, :], NQ,
                       rtmp.rearrange("p (b h f) -> p b h f", b=NB, h=NQ))
                dve.wait_ge(drained.sem, drained.upto(l, 5))
                k5 = kvraw[:, :, 0:P].rearrange("p b (h w f) -> p b h w f", h=NKV, w=2)
                o5 = krot[:, :, :, 0, :].rearrange("p b h (w f) -> p b h w f", w=2)
                rotate(k5[:, :, :, 0, :], k5[:, :, :, 1, :], o5[:, :, :, 0, :], o5[:, :, :, 1, :], NKV,
                       rtmp[:, 0:128].rearrange("p (b h f) -> p b h f", b=NB, h=NKV))
                dve.tensor_copy(krot[:, :, :, 1, :], krot[:, :, :, 0, :])
                dve.drain().then_inc(rot_done.sem, 1)

                dve.wait_ge(gates_turned.sem, gates_turned.upto(l, 1))
                R = [rows[0:NH, r, :] for r in range(6)]
                dve.tensor_copy(rows[0:NH, 0:2, :].rearrange("p r t -> p (r t)"), PS[0:NH, 7, :])
                dve.drain().then_inc(softplus_in.sem, 1)
                dve.wait_ge(softplus_out.sem, softplus_out.upto(l, 1))
                dve.scalar_tensor_tensor(out=R[1], in0=R[1], scalar=0.0, in1=R[5], op0=ALU.min, op1=ALU.subtract)
                dve.drain()
                dve.tensor_tensor_scan(R[5], ones[0:NH, 0:1].to_broadcast([NH, SEQ]), R[1], 0.0, ALU.mult, ALU.add)
                dve.drain()
                dve.tensor_tensor(R[2], R[0], R[5], ALU.subtract)
                dve.drain()
                dve.tensor_tensor_scan(R[3], R[2], R[2], 0.0, ALU.max, ALU.max)
                dve.drain()
                dve.scalar_tensor_tensor(out=R[4], in0=R[5], scalar=-1.0, in1=R[3], op0=ALU.mult, op1=ALU.subtract)
                dve.drain().then_inc(gate_rows.sem, 1)

                for i in range(2):
                    dve.wait_ge(qk_turned.sem, qk_turned.upto(l, i + 1))
                    dve.tensor_copy(qT[:, 4 * i:4 * i + 4, :].rearrange("p j t -> p (j t)"), bank(4 + 2 * i, 2)
                                    ).then_inc(qk_taken_dve.sem, 1)

                def soft(n):
                    b, h0, nh = BATCHES[n]
                    hs = slice(h0, h0 + nh)
                    dve.wait_ge(scored.sem, scored.upto(l, n + 1))
                    m = const("window")[:, 0:2 * P] if b == 1 else const("window")[:, P:2 * P]
                    pr = probs.rearrange("p (h s) -> p h s", h=nh)
                    for r in range(2):
                        dve.tensor_tensor(pr.rearrange("p (j r) s -> p r j s", r=2)[:, r],
                                          PS[:, 6 + r, :].rearrange("p (j s) -> p j s", j=nh // 2),
                                          bc(m.unsqueeze(1), [P, nh // 2, (b + 1) * P]), ALU.add)
                    dve.drain()
                    dve.tensor_reduce(mx[:, b, hs], pr, AX_X, ALU.max)
                    dve.drain()
                    dve.tensor_tensor(mx[:, b, hs], mx[:, b, hs], sinks8[:, hs], ALU.max)
                    dve.drain()
                    dve.tensor_scalar(nmx[:, b, hs], mx[:, b, hs], -DH ** -0.5, None, ALU.mult)
                    dve.drain()
                    dve.tensor_tensor(esink[:, b, hs], nmx[:, b, hs], sinks[:, 0, hs], ALU.add)
                    dve.drain().then_inc(masked.sem, 1)

                def take_probs(n):
                    b, h0, nh = BATCHES[n]
                    hs = slice(h0, h0 + nh)
                    dve.wait_ge(probs_turned.sem, probs_turned.upto(l, n + 1))
                    dve.tensor_copy(probsT, bank(4, 2)).then_inc(probs_taken.sem, 1)
                    dve.tensor_tensor(rinv[:, b, hs], rowsum[:, b, hs], esink[:, b, hs], ALU.add)
                    dve.drain()
                    dve.reciprocal(rinv[:, b, hs], rinv[:, b, hs])
                    dve.drain()

                def take_attended(n):
                    b, h0, nh = BATCHES[n]
                    dve.wait_ge(attended.sem, attended.upto(l, n + 1))
                    dve.tensor_tensor(hn[:, b, h0 * DH:(h0 + nh) * DH].rearrange("p (h d) -> p h d", h=nh),
                                      PS[:, 4, 0:nh * DH].rearrange("p (h d) -> p h d", h=nh),
                                      bc(rinv[:, b, h0:h0 + nh].unsqueeze(2), [P, nh, DH]), ALU.mult).then_inc(attn_taken.sem, 1)

                def convolve(i):
                    dve.wait_ge(drained.sem, drained.upto(l, 6 + i))
                    for m in range(4 * i, 4 * i + 4):
                        dve.memset(cout[:, m, 0:CONV - 1], 0.0)
                    dve.drain()
                    for j in range(CONV):
                        s = CONV - 1 - j
                        for m in range(4 * i, 4 * i + 4):
                            w = conv_w[:, j, m:m + 1]
                            if j == 0:
                                dve.tensor_scalar(cout[:, m, s:], cin[:, m, 0:SEQ - s], w, None, ALU.mult)
                            else:
                                dve.scalar_tensor_tensor(out=cout[:, m, s:], in0=cin[:, m, 0:SEQ - s], scalar=w,
                                                         in1=cout[:, m, s:], op0=ALU.mult, op1=ALU.add)
                        d = dve.drain()
                    d.then_inc(conved.sem, 1)

                for n in range(NBATCH):
                    soft(n)
                    if n == 4:
                        convolve(1)
                    take_probs(n)
                    if n == 1:
                        convolve(0)
                    take_attended(n)

                dve.wait_ge(m_spread.sem, m_spread.upto(l, 1))
                dve.tensor_copy(acol[:].rearrange("p b k h -> p (b k h)"), PS[:, 6, 0:16])
                dve.drain()
                mb = bank(4, 2).rearrange("p (h t) -> p h t", h=NH)
                for h in range(NH):
                    dve.tensor_scalar(mw[:, h, 0:SEQ], mb[:, h, :], acol[:, 0, 0, h:h + 1], 0.0, ALU.subtract, ALU.max)
                    dve.tensor_scalar(mw[:, h, SEQ:SEQ + P], mb[:, h, P:SEQ], acol[:, 1, 0, h:h + 1], 0.0, ALU.subtract, ALU.max)
                dve.drain().then_inc(m_exp_in.sem, 1)
                dve.wait_ge(m_exp_out.sem, m_exp_out.upto(l, 1))
                for a in (0, SEQ):
                    dve.tensor_tensor(mw[:, :, a:a + P], mw[:, :, a:a + P], bc(const("causal").unsqueeze(1), [P, NH, P]), ALU.mult)
                dve.drain()
                for i in range(2):
                    dve.wait_ge(m_scored.sem, m_scored.upto(l, i + 1))
                    base = 6 if i == 0 else 4
                    for j in range(2):
                        dve.scalar_tensor_tensor(out=mp[:, 2 * i + j, :], in0=PS[:, base + j, 0:SEQ + P], scalar=P ** -0.5,
                                                 in1=mw[:, 2 * i + j, :], op0=ALU.mult, op1=ALU.mult)
                dve.drain().then_inc(m_weighted.sem, 1)
                dve.wait_ge(m_out.sem, m_out.upto(l, 1))
                dn = den[:].rearrange("p b h -> p (b h)")
                dve.tensor_copy(dn, PS[:, 6, 0:NB * NH])
                dve.drain()
                dve.scalar_tensor_tensor(out=dn, in0=dn, scalar=-1.0, in1=dn, op0=ALU.mult, op1=ALU.max)
                dve.drain()
                dve.tensor_tensor(den[:], den[:], acol[:, :, 1, :], ALU.max)
                dve.drain()
                dve.reciprocal(dn, dn)
                dve.drain()
                ym = hn[:, :, 1536:2048]
                dve.tensor_tensor(ym.rearrange("p b (h n) -> p b h n", h=NH), PS[:, 4:6, :].rearrange("p b (h n) -> p b h n", h=NH),
                                  bc(den[:].unsqueeze(3), [P, NB, NH, P]), ALU.mult)
                dve.drain().then_inc(m_taken.sem, 1)

                dve.wait_ge(drained.sem, drained.upto(l, 10))
                dve.wait_ge(hgain_loaded.sem, hgain_loaded.upto(l, 16))
                dve.tensor_tensor(gsilu, gsilu, bc(hgain, [P, NB, 512]), ALU.mult)
                dve.wait_ge(hgrn_sq.sem, hgrn_sq.upto(l, 1))
                dve.tensor_reduce(hss[:], osq, AX_X, ALU.add)
                dve.drain()
                dve.tensor_scalar(hss[:], hss[:], 1.0 / P, EPS, ALU.mult, ALU.add).then_inc(hgrn_var.sem, 1)
                dve.wait_ge(hgrn_std.sem, hgrn_std.upto(l, 1))
                dve.reciprocal(hss[:], hss[:])
                dve.drain()
                yh = hn[:, :, 1024:1536]
                dve.tensor_tensor(yh.rearrange("p b (h n) -> p b h n", h=NH), PS[:, 4:6, :].rearrange("p b (h n) -> p b h n", h=NH),
                                  bc(hss[:].unsqueeze(3), [P, NB, NH, P]), ALU.mult)
                dve.drain()
                dve.tensor_tensor(yh, yh, gsilu, ALU.mult)
                dve.wait_ge(drained.sem, drained.upto(l, NS))
                dve.tensor_tensor(ym, ym, om_sig, ALU.mult)
                dve.drain().then_inc(mixed.sem, 1)
                dve.drain().then_inc(small_used.sem, 1)

                take_turned(l, 1)
                for o in range(NO):
                    dve.wait_ge(projected.sem, projected.upto(l, NS + o + 1))
                    r = xs[:, :, o * 512:(o + 1) * 512]
                    dve.tensor_tensor(r, r, pair(o), ALU.add).then_inc(out_taken.sem, 1)
                dve.drain().then_inc(x_ready.sem, 1)
                normalise(l, 1)
                take_turned(l, 2)

                def top16(vals, idx, src, spare):
                    dve.max(vals[:, 0:8], src)
                    dve.drain()
                    dve.max_index(idx[:, 0:8], vals[:, 0:8], src)
                    dve.match_replace(spare, vals[:, 0:8], src, -3.0e38)
                    dve.drain()
                    dve.max(vals[:, 8:16], spare)
                    dve.drain()
                    dve.max_index(idx[:, 8:16], vals[:, 8:16], spare)

                def choose(h, b):
                    if b == 0:
                        stop_until(dve, "dve", keyed.sem, keyed.upto(l, h + 1))
                    for s in range(2):
                        top16(topv[:, s, :], topi[:, s, :], PS[:, 5, (2 * b + s) * P:(2 * b + s + 1) * P], left[:, s, :])
                    dve.drain().then_inc(top_taken.sem, 1)
                    k3 = [P, TOPK, TOPK]
                    dve.tensor_tensor(cand.rearrange("p (i j) -> p i j", i=TOPK), bc(topv[:, 0, :].unsqueeze(2), k3),
                                      bc(topv[:, 1, :].unsqueeze(1), k3), ALU.add)
                    dve.tensor_copy(topif, topi)
                    dve.drain()
                    top16(tops[:], sel, cand, cand2)
                    dve.drain()
                    dve.tensor_scalar(gsum[:, 0:1], tops[:, 0:1], -1.0, None, ALU.mult).then_inc(tops_ready.sem, 1)
                    dve.tensor_scalar(selhl[:, 0, :], sel, 4, None, ALU.logical_shift_right)
                    dve.tensor_scalar(selhl[:, 1, :], sel, 15, None, ALU.bitwise_and)
                    dve.drain()
                    dve.tensor_copy(selhlf, selhl)
                    dve.drain()
                    for s in range(2):
                        dve.tensor_tensor(hot[:, s], bc(selhlf[:, s, :].unsqueeze(2), k3),
                                          bc(const("iota").unsqueeze(1), k3), ALU.is_equal)
                    dve.drain()
                    for s in range(2):
                        dve.tensor_tensor(hot[:, s], hot[:, s], bc(topif[:, s, :].unsqueeze(1), k3), ALU.mult)
                    dve.drain()
                    dve.tensor_reduce(selidx, hot, AX_X, ALU.add)
                    dve.drain()
                    dve.scalar_tensor_tensor(out=idxf, in0=selidx[:, 0, :], scalar=float(NKEYS), in1=selidx[:, 1, :],
                                             op0=ALU.mult, op1=ALU.add)
                    dve.drain()
                    dve.tensor_scalar(idx_u[b][:], idxf, layer_base[:, 0:1], None, ALU.add)
                    dve.drain().then_inc(idx_ready.sem, 1)
                    dve.wait_ge(gate_exped.sem, l * GROUPS + h * NB + b + 1)
                    dve.reciprocal(gsum[:, 1:2], gsum[:, 1:2])
                    dve.drain()
                    dve.tensor_scalar(gate[:, b, :], texp, gsum[:, 1:2], None, ALU.mult)
                    dve.drain()

                def v_indices(h, b):
                    dve.tensor_copy(idx_v[b][:], idx_u[b][:]).then_inc(vidx_ready.sem, 1)

                def dots(h, b, ks):
                    g = h * NB + b
                    for k in ks:
                        dve.wait_ge(u_loaded[k % RING].sem, ((l * GROUPS + g) * (TOPK // RING) + k // RING) * 16 + 16)
                        r = urow[k % RING]
                        dve.tensor_tensor_reduce(r, r, hn[:, b, :], 1.0, 0.0, ALU.mult, ALU.add, pre[:, b, k:k + 1]
                                                 ).then_inc(u_free.sem, 1)

                def activate(h, b):
                    dve.drain().then_inc(dotted.sem, 1)
                    dve.wait_ge(gelued.sem, l * GROUPS + h * NB + b + 1)
                    dve.tensor_tensor(act_k[:, b, :], act_k[:, b, :], gate[:, b, :], ALU.mult).then_inc(act_ready.sem, 1)

                def take_sum(h, b):
                    dve.wait_ge(v_free.sem, (l * GROUPS + h * NB + b + 1) * TOPK + RING)
                    dve.tensor_tensor(xs[:, b, :], xs[:, b, :], bank(0, 4), ALU.add)
                    dve.drain().then_inc(sum_taken.sem, 1)

                choose(0, 0)
                choose(0, 1)
                v_indices(0, 0)
                dots(0, 0, range(TOPK))
                activate(0, 0)
                with dve.Fori(0, HEADS - 1) as h:
                    dots(h, 1, range(0, 8))
                    choose(h + 1, 0)
                    v_indices(h, 1)
                    dots(h, 1, range(8, TOPK))
                    activate(h, 1)
                    take_sum(h, 0)
                    dots(h + 1, 0, range(0, 6))
                    choose(h + 1, 1)
                    v_indices(h + 1, 0)
                    dots(h + 1, 0, range(6, TOPK))
                    activate(h + 1, 0)
                    take_sum(h, 1)
                v_indices(HEADS - 1, 1)
                dots(HEADS - 1, 1, range(TOPK))
                activate(HEADS - 1, 1)
                take_sum(HEADS - 1, 0)
                take_sum(HEADS - 1, 1)
                dve.tensor_scalar(layer_base[:], layer_base[:], float(EXPERTS), None, ALU.add)
                dve.drain().then_inc(x_ready.sem, 1)

            normalise(DEPTH, 0)


_INS = ["x", "norm_mix", "w_in", "w_out", "attn_sinks", "hgrn_lb_logits", "hgrn_out_norm", "mlstm_conv", "mlstm_i_bias",
        "mlstm_f_bias", "norm_ffn", "peer_query", "peer_sub_keys", "peer_u", "peer_v", "norm_final"]


def kernel(**inputs):
    import numpy as _np
    import concourse.bacc as _bacc
    from concourse import mybir as _mybir
    from concourse.bass_utils import run_bass_kernel_spmd as _run

    nc = _bacc.Bacc("TRN2", target_bir_lowering=False, num_devices=1)
    arrays, args = {}, []
    for name in _INS:
        arrays[f"in_{name}_dram"] = _np.ascontiguousarray(inputs[name])
    arrays["consts_dram"] = constants()
    for name, a in arrays.items():
        args.append(nc.dram_tensor(name, a.shape, _mybir.dt.from_np(a.dtype), kind="ExternalInput").ap())
    out = nc.dram_tensor("out_dram", (1, SEQ, D), F32, kind="ExternalOutput").ap()
    trunk(nc, *args, out)
    r = _run(nc, [arrays], core_ids=[0])
    return r.results[0]["out_dram"]
```

```python
from contextlib import ExitStack

import numpy as np

import concourse.bass as bass
from concourse import mybir

ALU = mybir.AluOpType
ACT = mybir.ActivationFunctionType
F32 = mybir.dt.float32
F32R = mybir.dt.float32r
U32 = mybir.dt.uint32
I32 = mybir.dt.int32
AX_X = mybir.AxisListType.X

P = 128
SEQ, D, DEPTH = 256, 2048, 2
NB = SEQ // P
NC = D // P
EPS, NEG, TINY = 1e-6, -1e30, 1e-30
DH, NQ, NKV = 64, 16, 2
NH = 4
CONV = 4
HEADS, NKEYS, TOPK = 8, 128, 16
EXPERTS = NKEYS * NKEYS
FLOOR = 2.0 ** -60

COLS = dict(qa=0, ka=1024, va=1152, qh=1280, fh=1792, ih=2304, gh=2816, qkm=3328, vm=4352, om=4864, gates=5376)
SLABS = [("fh", COLS["fh"], 512), ("qh", COLS["qh"], 512), ("kv", COLS["ka"], 256 + 2 * NH), ("qa0", 0, 512),
         ("qa1", 512, 512), ("qkm0", COLS["qkm"], 512), ("qkm1", COLS["qkm"] + 512, 512),
         ("ih", COLS["ih"], 512), ("vm", COLS["vm"], 512), ("gh", COLS["gh"], 512), ("om", COLS["om"], 512)]
NS = len(SLABS)
KV = [name for name, _, _ in SLABS].index("kv")
NO = D // 512
QC = NC // 4
IN_PIECES, PIECES = 4 * NS, 4 * (NS + NO)
RAWS, HIS, LOS = 2, 3, 2
LEVELS = [64, 32, 16, 8, 4, 2, 1]
NL = len(LEVELS)
LEVEL_STEP = [9] + [10 + i for i in range(1, NL + 1)]
BATCHES = [(1, 0, 4), (1, 4, 4), (1, 8, 4), (1, 12, 4), (0, 0, 8), (0, 8, 8)]
NBATCH = len(BATCHES)
GROUPS = HEADS * NB
RING = 4
VECTOR_SLOTS = range(1, TOPK, RING)
V_SUMS = GROUPS * TOPK - len(VECTOR_SLOTS)


def summed(k):
    return (GROUPS - 1) * TOPK + k - len([i for i in VECTOR_SLOTS if i < k])


CONST = {}
_at = 0
for _name, _n in (("ident", P), ("causal", P), ("levels", NL * P), ("window", 2 * P), ("cos", NB * 32),
                  ("sin", NB * 32), ("pick", NH * P), ("iota", TOPK)):
    CONST[_name] = (_at, _at + _n)
    _at += _n
NCONST = _at


def constants():
    c = np.zeros((P, NCONST), np.float32)
    i, j = np.arange(P)[:, None], np.arange(P)[None, :]

    def put(name, value):
        a, b = CONST[name]
        c[:, a:b] = value

    put("ident", i == j)
    put("causal", i <= j)
    put("levels", np.concatenate([(i // (2 * L) == j // (2 * L)) & (i % (2 * L) < L) & (j % (2 * L) >= L)
                                  for L in LEVELS], axis=1))
    window = np.concatenate([np.where(j > i, 0.0, NEG), np.where(j <= i, 0.0, NEG)], axis=1)
    put("window", window)
    half = DH // 2
    inv = (np.float32(10000.0) ** (-np.arange(half, dtype=np.float32) / np.float32(half))).astype(np.float32)
    ang = (np.arange(SEQ, dtype=np.float32)[:, None] * inv[None, :]).astype(np.float32)
    for name, f in (("cos", np.cos), ("sin", np.sin)):
        put(name, f(ang.astype(np.float64)).reshape(NB, P, half).transpose(1, 0, 2).reshape(P, NB * half))
    a, _ = CONST["pick"]
    for h in range(NH):
        c[h, a + h * P:a + (h + 1) * P] = 1.0
    put("iota", np.arange(TOPK)[None, :])
    return c


class Signal:

    def __init__(self, sem, per_layer, start=0):
        self.sem, self.per_layer, self.start = sem, per_layer, start

    def upto(self, layer, n):
        return layer * self.per_layer + (n + self.start)


def trunk(nc, x, norm_mix, w_in, w_out, attn_sinks, hgrn_lb_logits, hgrn_out_norm, mlstm_conv, mlstm_i_bias,
          mlstm_f_bias, norm_ffn, peer_query, peer_sub_keys, peer_u, peer_v, norm_final, consts, out):
    with ExitStack() as ctx:
        def sb(name, shape, dt=F32):
            return ctx.enter_context(nc.sbuf_tensor(name, shape, dt))

        def signal(name, per_layer, start=0):
            return Signal(ctx.enter_context(nc.semaphore(name)), per_layer, start)

        cst = sb("cst", [P, NCONST])
        xs = sb("xs", [P, NB, D])
        hn = sb("hn", [P, NB, D])
        hT = [sb(f"hT_{part}", [P, NC, SEQ]) for part in ("hi", "lo")]
        raw0 = sb("raw0", [P, QC * 512])
        hi = [sb(f"hi{i}", [P, QC * 512]) for i in range(HIS)]
        lo = [sb(f"lo{i}", [P, QC * 512]) for i in range(LOS)]
        keysT = sb("keysT", [P, 2 * HEADS, NKEYS])
        gain = sb("gain", [P, D])
        work = sb("work", [P, 4 * NC * 256])
        PS = ctx.enter_context(nc.psum_tensor("PS", [P, 8, 512], F32))

        ones = sb("ones", [P, P])
        diag = sb("diag", [P, RING, P])
        lb_rows = sb("lb_rows", [DEPTH * NH, P])
        conv_rows = sb("conv_rows", [CONV * 2 * NH, P])
        conv_w = sb("conv_w", [P, CONV, 2 * NH])
        lb_all = sb("lb_all", [P, 2, DEPTH, NH])
        lb = sb("lb", [P, 2, NH])
        lbt = sb("lbt", [P, 4, NH])
        sinks = sb("sinks", [P, 1, NQ])
        sinks8 = sb("sinks8", [P, NQ])
        gate_bias = sb("gate_bias", [P, 1, 2 * NH])
        ss = sb("ss", [P, NB])
        rms = sb("rms", [P, NB])
        rstd = sb("rstd", [P, NB])
        mx = sb("mx", [P, NB, NQ])
        nmx = sb("nmx", [P, NB, NQ])
        rowsum = sb("rowsum", [P, NB, NQ])
        esink = sb("esink", [P, NB, NQ])
        rinv = sb("rinv", [P, NB, NQ])
        gnat = sb("gnat", [P, NB, 2 * NH])
        acol = sb("acol", [P, NB, 2, NH])
        den = sb("den", [P, NB, NH])
        hss = sb("hss", [P, NB, NH])
        layer_base = sb("layer_base", [P, 1])
        idx_u = [sb(f"idx_u{b}", [P, TOPK], U32) for b in range(NB)]
        idx_v = [sb(f"idx_v{b}", [P, TOPK], U32) for b in range(NB)]
        gate = sb("gate", [P, NB, TOPK])
        pre = sb("pre", [P, NB, TOPK])
        act_k = sb("act_k", [P, NB, TOPK])
        tops = sb("tops", [P, TOPK])
        gsum = sb("gsum", [P, 2])

        def const(name):
            a, b = CONST[name]
            return cst[:, a:b]

        ident = const("ident")

        def region(a, n):
            assert a + n <= 4 * NC * 256
            return work[:, a:a + n]

        silq = region(0, 1024).rearrange("p (h t) -> p h t", h=NH)
        kk = region(1024, 1024).rearrange("p (h t) -> p h t", h=NH)
        cum = region(2048, 1024).rearrange("p (h t) -> p h t", h=NH)
        wts = [region(3072 + 1024 * i, 1024).rearrange("p (h t) -> p h t", h=NH) for i in range(2)]
        qa_w = region(5120, 1024).rearrange("p (h t) -> p h t", h=NH)
        kk_w = region(6144, 1024).rearrange("p (h t) -> p h t", h=NH)
        hsc = region(7168, 1536).rearrange("p (k h t) -> p k h t", h=NH, k=3)
        kvraw = region(8704, 512).rearrange("p (b n) -> p b n", b=NB)
        qraw = region(9216, 2048).rearrange("p (b n) -> p b n", b=NB)
        cin = region(11264, 2048).rearrange("p (m t) -> p m t", m=2 * NH)
        cout = region(13312, 2048).rearrange("p (m t) -> p m t", m=2 * NH)
        vh = keysT[:, 8:16, :].rearrange("p a n -> p (a n)").rearrange("p (b n) -> p b n", b=NB)
        hgain = keysT[:, 0:4, :].rearrange("p a n -> p (a n)").unsqueeze(1)
        qrot = region(0, 2048).rearrange("p (b n) -> p b n", b=NB)
        krot = region(2048, 512).rearrange("p (b k d n) -> p b k d n", b=NB, k=NKV, d=2)
        rtmp = region(4096, 512)
        rows = region(2560, 1536).rearrange("p (r t) -> p r t", r=6)
        qT = region(4096, 2048).rearrange("p (j t) -> p j t", j=NQ // 2)
        kT = region(6144, 512).rearrange("p (k t) -> p k t", k=NKV)
        probs = region(0, 1024)
        probsT = region(9216, 1024)
        gsilu = region(10240, 1024).rearrange("p (b n) -> p b n", b=NB)
        vaug = region(15360, 1024).rearrange("p (b h n) -> p b h n", b=NB, h=NH)
        mw = region(1024, 1536).rearrange("p (h t) -> p h t", h=NH)
        mp = region(2560, 1536).rearrange("p (h t) -> p h t", h=NH)
        osq = region(4096, 1024).rearrange("p (b h n) -> p b h n", b=NB, h=NH)
        om_sig = region(5120, 1024).rearrange("p (b n) -> p b n", b=NB)
        urow = [region(i * D, D) for i in range(RING)]
        vrow = [region((RING + i) * D, D) for i in range(RING)]
        raw = [raw0, gain]
        keys = region(7 * D, D).rearrange("p (a n) -> p a n", a=2 * HEADS)
        qpT = gain[:, 0:512]
        tk = gain[:, 512:2048]
        topv = tk[:, 0:32].rearrange("p (s k) -> p s k", s=2)
        topi = tk[:, 32:64].bitcast(U32).rearrange("p (s k) -> p s k", s=2)
        topif = tk[:, 64:96].rearrange("p (s k) -> p s k", s=2)
        sel = tk[:, 96:112].bitcast(U32)
        selhl = tk[:, 112:144].bitcast(U32).rearrange("p (s k) -> p s k", s=2)
        selhlf = tk[:, 144:176].rearrange("p (s k) -> p s k", s=2)
        selidx = tk[:, 176:208].rearrange("p (s k) -> p s k", s=2)
        idxf = tk[:, 208:224]
        texp = tk[:, 224:240]
        left = tk[:, 240:496].rearrange("p (s n) -> p s n", s=2)
        cand = tk[:, 496:752]
        cand2 = tk[:, 752:1008]
        hot = tk[:, 1008:1520].rearrange("p (s k j) -> p s k j", s=2, k=TOPK)

        def pair(j):
            return PS[:, 2 * (j % 2):2 * (j % 2) + 2, :]

        def turn_order(use):
            return [(g, b) for g in range(4) for b in range(NB)] if use == 1 else [(g, b) for b in range(NB) for g in range(4)]

        def bank(i, n=1):
            return PS[:, i:i + n, :].rearrange("p b n -> p (b n)")

        const_loaded = signal("const_loaded", 0)
        x_loaded = signal("x_loaded", 0)
        gain_loaded = signal("gain_loaded", 2 * 16)
        gain_used = signal("gain_used", 2, start=1)
        small_loaded = signal("small_loaded", 4 * 16)
        hgain_loaded = signal("hgain_loaded", 16)
        small_used = signal("small_used", 1, start=1)
        raw_loaded = [signal(f"raw{i}_loaded", (PIECES // RAWS + 2) * 16) for i in range(RAWS)]
        hi_ready = signal("hi_ready", PIECES)
        lo_ready = signal("lo_ready", PIECES)
        pieces_used = signal("pieces_used", PIECES, start=1)
        wq_loaded = signal("wq_loaded", 2 * HEADS * 16)
        wq_hi_ready = signal("wq_hi_ready", 2 * HEADS)
        wq_lo_ready = signal("wq_lo_ready", 2 * HEADS, start=1)
        keys_loaded = signal("keys_loaded", 2 * HEADS * 16)
        x_ready = signal("x_ready", 2)
        sumsq_ready = signal("sumsq_ready", 2)
        var_ready = signal("var_ready", 2)
        std_ready = signal("std_ready", 2)
        normed = signal("normed", 2 * NB * 2)
        turned = signal("turned", 3 * 8)
        turned_dve = signal("turned_dve", 3 * 8)
        turned_act = signal("turned_act", 3 * 8)
        setup_turned = signal("setup_turned", 0)
        logits_ready = signal("logits_ready", 0)
        logits_exped = signal("logits_exped", 0)
        conv_turned = signal("conv_turned", 1)
        conv_ready = signal("conv_ready", 1)
        drained = signal("drained", NS)
        ln_args = signal("ln_args", 1)
        ln_ready = signal("ln_ready", 1)
        level_diff = signal("level_diff", NL + 1)
        level_exp = signal("level_exp", NL + 1)
        level_ops = signal("level_ops", NL + 1)
        level_scored = signal("level_scored", NL + 1)
        level_taken = signal("level_taken", NL + 1)
        gates_nat = signal("gates_nat", 1)
        gates_turned = signal("gates_turned", 1)
        softplus_in = signal("softplus_in", 1)
        softplus_out = signal("softplus_out", 1)
        gate_rows = signal("gate_rows", 1)
        rot_done = signal("rot_done", 1)
        qk_turned = signal("qk_turned", 3)
        qk_taken_dve = signal("qk_taken_dve", 2)
        qk_taken_act = signal("qk_taken_act", 1)
        scored = signal("scored", NBATCH)
        masked = signal("masked", NBATCH)
        exped = signal("exped", NBATCH)
        probs_turned = signal("probs_turned", NBATCH)
        probs_taken = signal("probs_taken", NBATCH)
        attended = signal("attended", NBATCH)
        attn_taken = signal("attn_taken", NBATCH)
        conved = signal("conved", 4)
        silued = signal("silued", 1)
        m_spread = signal("m_spread", 1)
        m_exp_in = signal("m_exp_in", 1)
        m_exp_out = signal("m_exp_out", 1)
        m_scored = signal("m_scored", 2)
        m_weighted = signal("m_weighted", 1)
        m_out = signal("m_out", 1)
        m_taken = signal("m_taken", 1)
        hgrn_out = signal("hgrn_out", 1)
        hgrn_sq = signal("hgrn_sq", 1)
        hgrn_var = signal("hgrn_var", 1)
        hgrn_std = signal("hgrn_std", 1)
        mixed = signal("mixed", 2)
        out_taken = signal("out_taken", NO)
        keys_turned = signal("keys_turned", 4)
        keys_taken = signal("keys_taken", 4)
        query_done = signal("query_done", 2 * HEADS, start=1)
        query_taken = signal("query_taken", HEADS)
        keyed = signal("keyed", HEADS, start=1)
        top_taken = signal("top_taken", GROUPS, start=1)
        tops_ready = signal("tops_ready", GROUPS)
        gate_exped = signal("gate_exped", GROUPS)
        idx_ready = signal("idx_ready", GROUPS)
        vidx_ready = signal("vidx_ready", GROUPS, start=1)
        u_loaded = [signal(f"u_loaded{i}", GROUPS * TOPK // RING * 16) for i in range(RING)]
        v_loaded = [signal(f"v_loaded{i}", GROUPS * TOPK // RING * 16) for i in range(RING)]
        u_free = signal("u_free", GROUPS * TOPK, start=RING)
        v_free = signal("v_free", V_SUMS, start=RING)
        v_added = signal("v_added", len(VECTOR_SLOTS))
        dotted = signal("dotted", GROUPS)
        gelued = signal("gelued", GROUPS)
        act_ready = signal("act_ready", GROUPS)
        diag_ready = signal("diag_ready", V_SUMS)
        sum_taken = signal("sum_taken", GROUPS, start=1)
        stored = signal("stored", 0)

        waits = {e: signal(f"waits_{e}", 0) for e in ("sp", "pe", "dve", "pool")}

        block = ctx.enter_context(nc.Block())

        def stop_until(engine, name, sem, value):
            engine.wait_ge(sem, value)
            engine.sem_inc(waits[name].sem, 1)

        def layer_of(t, l):
            return t[bass.ds(l, 1)]

        @block.sync
        def _(sp):
            sp.dma_start(cst[:], consts).then_inc(const_loaded.sem, 16)
            sp.dma_start(lb_rows[:], hgrn_lb_logits.rearrange("l (h p) -> (l h) p", p=P)).then_inc(const_loaded.sem, 16)
            sp.dma_start(xs[:], x.rearrange("a (b p) d -> p (a b) d", p=P)).then_inc(x_loaded.sem, 16)

            with sp.Fori(0, DEPTH) as l:
                def load_piece(p):
                    j, q = p // 4, p % 4
                    mat, c0, n = (w_in, SLABS[j][1], SLABS[j][2]) if j < NS else (w_out, (j - NS) * 512, 512)
                    if p >= RAWS:
                        stop_until(sp, "sp", lo_ready.sem, lo_ready.upto(l, p - RAWS + 1))
                    dst = raw[p % RAWS][:, 0:QC * n].rearrange("p (c n) -> p c n", c=QC)
                    src = layer_of(mat, l)[:, q * QC * P:(q + 1) * QC * P, :].rearrange("a (c p) n -> p (a c) n", p=P)
                    m = n if j != KV else 2 * P
                    sp.dma_start(dst[:, :, 0:m], src[:, :, c0:c0 + m]).then_inc(raw_loaded[p % RAWS].sem, 16)
                    if j == KV:
                        g = COLS["gates"]
                        sp.dma_start(dst[:, :, m:n], src[:, :, g:g + 2 * NH]).then_inc(raw_loaded[p % RAWS].sem, 16)

                stop_until(sp, "sp", vidx_ready.sem, vidx_ready.upto(l, 0))
                sp.dma_start(gain[:].unsqueeze(1), layer_of(norm_mix, l).partition_broadcast(P)).then_inc(gain_loaded.sem, 16)
                stop_until(sp, "sp", wq_lo_ready.sem, wq_lo_ready.upto(l, 0))
                load_piece(0)
                stop_until(sp, "sp", small_used.sem, small_used.upto(l, 0))
                sp.dma_start(conv_rows[:], layer_of(mlstm_conv, l).rearrange("a j (m p) -> (a j m) p", p=P)).then_inc(small_loaded.sem, 16)
                sp.dma_start(sinks[:], layer_of(attn_sinks, l).partition_broadcast(P)).then_inc(small_loaded.sem, 16)
                sp.dma_start(gate_bias[:, :, 0:NH], layer_of(mlstm_i_bias, l).partition_broadcast(P)).then_inc(small_loaded.sem, 16)
                sp.dma_start(gate_bias[:, :, NH:2 * NH], layer_of(mlstm_f_bias, l).partition_broadcast(P)).then_inc(small_loaded.sem, 16)
                sp.dma_start(hgain, layer_of(hgrn_out_norm, l).partition_broadcast(P)).then_inc(hgain_loaded.sem, 16)
                stop_until(sp, "sp", gain_used.sem, gain_used.upto(l, 1))
                for p in range(1, IN_PIECES + 4):
                    load_piece(p)
                stop_until(sp, "sp", mixed.sem, mixed.upto(l, 2))
                for s in range(2):
                    for h in range(HEADS):
                        sp.dma_start(keys[:, s * HEADS + h, :], layer_of(peer_sub_keys, l)[:, s, h].rearrange("a n d -> (a n) d")
                                     ).then_inc(keys_loaded.sem, 16)
                for p in range(IN_PIECES + 4, PIECES):
                    load_piece(p)

                def load_query(h, s):
                    sp.dma_start(raw0[:].rearrange("p (c n) -> p c n", c=NC), layer_of(peer_query, l)[:, :, bass.ds(h * 256 + s * P, P)]
                                 .rearrange("a (c p) n -> p (a c) n", p=P)).then_inc(wq_loaded.sem, 16)

                stop_until(sp, "sp", lo_ready.sem, lo_ready.upto(l, PIECES - 1))
                load_query(0, 0)
                stop_until(sp, "sp", lo_ready.sem, lo_ready.upto(l, PIECES))
                sp.dma_start(gain[:].unsqueeze(1), layer_of(norm_ffn, l).partition_broadcast(P)).then_inc(gain_loaded.sem, 16)
                stop_until(sp, "sp", wq_lo_ready.sem, wq_lo_ready.upto(l, 1))
                load_query(0, 1)
                with sp.Fori(0, HEADS - 1) as h:
                    for s in range(2):
                        stop_until(sp, "sp", wq_lo_ready.sem, wq_lo_ready.upto(l, 2 * h + s + 2))
                        load_query(h + 1, s)

            stop_until(sp, "sp", vidx_ready.sem, vidx_ready.upto(DEPTH, 0))
            sp.dma_start(gain[:], norm_final.partition_broadcast(P)).then_inc(gain_loaded.sem, 16)
            for b in range(NB):
                sp.wait_ge(normed.sem, normed.upto(DEPTH, 2 * (b + 1)))
                sp.dma_start(out[0, b * P:(b + 1) * P, :], hn[:, b, :]).then_inc(stored.sem, 16)
            sp.wait_ge(stored.sem, 16 * NB)

        @block.tensor
        def _(pe):
            for s in (pieces_used, query_done, keyed):
                pe.sem_inc(s.sem, s.start)
            pe.wait_ge(const_loaded.sem, 32)
            pe.transpose(PS[:, 7, 0:DEPTH * NH], lb_rows[:], ident[0:DEPTH * NH, 0:DEPTH * NH]).then_inc(setup_turned.sem, 1)

            def turn(l, use, src):
                for f in range(8):
                    if f >= 4:
                        pe.wait_ge(turned_dve.sem, turned_dve.upto(l, 8 * use + f - 3))
                    g, b = turn_order(use)[f]
                    if use == 1:
                        if g == 3 and b == 0:
                            pe.wait_ge(mixed.sem, mixed.upto(l, 2))
                    elif g % 2 == 0:
                        pe.wait_ge(normed.sem, normed.upto(l, (use // 2 * NB + b) * 2 + g // 2 + 1))
                    for i in range(4):
                        c = 4 * g + i
                        t = pe.transpose(PS[:, 4 + f % 4, i * P:(i + 1) * P], src[:, b, c * P:(c + 1) * P], ident)
                    t.then_inc(turned.sem, 1)
                pe.wait_ge(turned_dve.sem, turned_dve.upto(l, 8 * use + 8))

            def products(dst, left, right, first, last):
                for i, (a, b) in enumerate(((0, 0), (0, 1), (1, 0))):
                    mm = pe.matmul(dst, left[a], right[b], start=(first and i == 0), stop=(last and i == 2))
                return mm

            def project(l, p):
                j, q = p // 4, p % 4
                name, _, n = SLABS[j] if j < NS else ("w_out", 0, 512)
                pe.wait_ge(lo_ready.sem, lo_ready.upto(l, p + 1))
                w = [m[:, 0:QC * n].rearrange("p (c n) -> p c n", c=QC).bitcast(F32R) for m in (hi[p % HIS], lo[p % LOS])]
                h = [m[:].bitcast(F32R) for m in hT]
                dst = pair(j)
                for i in range(QC):
                    c = QC * q + i
                    first, last = c == 0, c == NC - 1
                    if name in ("fh", "qh", "qkm0", "qkm1"):
                        d = dst.rearrange("p b (m t) -> p (b m) t", m=2)
                        for m in range(4):
                            mm = products(d[:, m, :], [x[:, i, m * P:(m + 1) * P] for x in w], [x[:, c, :] for x in h],
                                          first and m % 2 == 0, last and m % 2 == 1)
                    else:
                        for b in range(NB):
                            mm = products(dst[:, b, 0:n], [x[:, c, b * P:(b + 1) * P] for x in h], [x[:, i, :] for x in w], first, last)
                mm.then_inc(pieces_used.sem, 1)

            with pe.Fori(0, DEPTH) as l:
                def nothing():
                    pass

                def conv_weights():
                    stop_until(pe, "pe", small_loaded.sem, small_loaded.upto(l, 4 * 16))
                    pe.transpose(PS[:, 7, 0:CONV * 2 * NH], conv_rows[:], ident[0:CONV * 2 * NH, 0:CONV * 2 * NH]).then_inc(conv_turned.sem, 1)

                def level(i):
                    if i == NL:
                        pe.wait_ge(level_taken.sem, level_taken.upto(l, NL))
                        d = bank(4, 2).rearrange("p (b h t) -> p b h t", h=NH, b=NB)
                        for h in range(NH):
                            for b in range(NB):
                                r = slice(b * P, (b + 1) * P)
                                mm = pe.matmul(d[:, b, h, :], kk[:, h, r], silq[:, h, r], start=True, stop=True)
                        pe.wait_ge(level_ops.sem, level_ops.upto(l, NL + 1))
                        for h in range(NH):
                            mm = pe.matmul(PS[:, 6, h * P:(h + 1) * P], kk_w[:, h, 0:P], qa_w[:, h, P:SEQ], start=True, stop=True)
                    else:
                        if i > 1:
                            pe.wait_ge(level_taken.sem, level_taken.upto(l, i - 1))
                        pe.wait_ge(level_ops.sem, level_ops.upto(l, i + 1))
                        L = LEVELS[i]
                        d = PS[:, 4 + i % 2, :].rearrange("p (b h g u) -> p b h g u", h=NH, b=NB, u=L)
                        for h in range(NH):
                            for b in range(NB):
                                q = qa_w[:, h, b * P:(b + 1) * P].rearrange("p (g u) -> p g u", u=2 * L)[:, :, L:2 * L]
                                mm = pe.matmul(d[:, b, h], kk_w[:, h, b * P:(b + 1) * P], q, start=True, stop=True)
                    mm.then_inc(level_scored.sem, 1)

                def gate_turn():
                    pe.wait_ge(gates_nat.sem, gates_nat.upto(l, 1))
                    for k in range(2):
                        for b in range(NB):
                            mm = pe.transpose(PS[0:NH, 7, k * SEQ + b * P:k * SEQ + (b + 1) * P], gnat[:, b, k * NH:(k + 1) * NH], ident)
                    mm.then_inc(gates_turned.sem, 1)

                def turn_q():
                    pe.wait_ge(rot_done.sem, rot_done.upto(l, 1))
                    pe.wait_ge(level_taken.sem, level_taken.upto(l, NL + 1))
                    pe.wait_ge(gate_rows.sem, gate_rows.upto(l, 1))
                    d = bank(4, 4).rearrange("p (j t) -> p j t", j=NQ // 2)
                    for j in range(NQ // 2):
                        for b in range(NB):
                            mm = pe.transpose(d[:, j, b * P:(b + 1) * P], qrot[:, b, j * P:(j + 1) * P], ident)
                        if j % 4 == 3:
                            mm.then_inc(qk_turned.sem, 1)

                def turn_k():
                    pe.wait_ge(qk_taken_dve.sem, qk_taken_dve.upto(l, 1))
                    for k in range(NKV):
                        for b in range(NB):
                            mm = pe.transpose(PS[:, 4, (2 * k + b) * P:(2 * k + b + 1) * P],
                                              krot[:, b, k].rearrange("p d n -> p (d n)"), ident)
                    mm.then_inc(qk_turned.sem, 1)

                def scores(n):
                    b, h0, nh = BATCHES[n]
                    if n == 0:
                        pe.wait_ge(qk_taken_dve.sem, qk_taken_dve.upto(l, 2))
                        pe.wait_ge(qk_taken_act.sem, qk_taken_act.upto(l, 1))
                    else:
                        pe.wait_ge(masked.sem, masked.upto(l, n))
                    keys_n = (b + 1) * P
                    d = PS[:, 6:8, :].rearrange("p r (j s) -> p r j s", j=nh // 2)
                    for i in range(nh):
                        h = h0 + i
                        r = slice(DH * (h % 2), DH * (h % 2) + DH)
                        mm = pe.matmul(d[:, i % 2, i // 2, :], qT[r, h // 2, b * P:(b + 1) * P], kT[r, h // (NQ // NKV), 0:keys_n],
                                       start=True, stop=True)
                    mm.then_inc(scored.sem, 1)

                def turn_probs(n):
                    b, h0, nh = BATCHES[n]
                    pe.wait_ge(exped.sem, exped.upto(l, n + 1))
                    if n > 0:
                        pe.wait_ge(attn_taken.sem, attn_taken.upto(l, n))
                    d = bank(4, 2).rearrange("p (k t) -> p k t", k=8)
                    pr = probs.rearrange("p (k s) -> p k s", k=8)
                    for k in range(8):
                        mm = pe.transpose(d[:, k, :], pr[:, k, :], ident)
                    mm.then_inc(probs_turned.sem, 1)

                def attend(n):
                    b, h0, nh = BATCHES[n]
                    pe.wait_ge(probs_taken.sem, probs_taken.upto(l, n + 1))
                    pt = probsT.rearrange("p (k t) -> p k t", k=8)
                    for i in range(nh):
                        kv = (h0 + i) // (NQ // NKV)
                        for kb in range(b + 1):
                            mm = pe.matmul(PS[:, 4, i * DH:(i + 1) * DH], pt[:, i * (b + 1) + kb, :],
                                           kvraw[:, kb, P + kv * DH:P + (kv + 1) * DH], start=(kb == 0), stop=(kb == b))
                    mm.then_inc(attended.sem, 1)

                def spread_m():
                    pe.wait_ge(attn_taken.sem, attn_taken.upto(l, NBATCH))
                    a, _ = CONST["pick"]
                    d = bank(4, 2).rearrange("p (h t) -> p h t", h=NH)
                    for h in range(NH):
                        pe.matmul(d[:, h, :], cst[0:NH, a + h * P:a + (h + 1) * P], rows[0:NH, 3, :], start=True, stop=True)
                    for b in range(NB):
                        for k, r in ((0, 2), (1, 4)):
                            mm = pe.transpose(PS[:, 6, (2 * b + k) * NH:(2 * b + k + 1) * NH],
                                              rows[0:NH, r, b * P:(b + 1) * P], ident[0:NH, 0:NH])
                    mm.then_inc(m_spread.sem, 1)

                def m_scores(i):
                    pe.wait_ge(silued.sem, silued.upto(l, 1))
                    pe.wait_ge(m_exp_in.sem, m_exp_in.upto(l, 1))
                    base = 6 if i == 0 else 4
                    for j in range(2):
                        h = 2 * i + j
                        pe.matmul(PS[:, base + j, 0:SEQ], cout[:, NH + h, 0:P], cout[:, h, :], start=True, stop=True)
                        mm = pe.matmul(PS[:, base + j, SEQ:SEQ + P], cout[:, NH + h, P:SEQ], cout[:, h, P:SEQ], start=True, stop=True)
                    mm.then_inc(m_scored.sem, 1)

                def m_attend():
                    pe.wait_ge(m_weighted.sem, m_weighted.upto(l, 1))
                    pe.wait_ge(drained.sem, drained.upto(l, 9))
                    for b in range(NB):
                        for h in range(NH):
                            for kb in range(b + 1):
                                w = mp[:, h, b * P:(b + 1) * P] if kb == 0 else mp[:, h, SEQ:SEQ + P]
                                pe.matmul(PS[:, 4 + b, h * P:(h + 1) * P], w, vaug[:, kb, h, :], start=(kb == 0), stop=(kb == b))
                    for b in range(NB):
                        for h in range(NH):
                            for kb in range(b + 1):
                                w = mp[:, h, b * P:(b + 1) * P] if kb == 0 else mp[:, h, SEQ:SEQ + P]
                                mm = pe.matmul(PS[:, 6, b * NH + h:b * NH + h + 1], w, ones[:, 0:1], start=(kb == 0), stop=(kb == b))
                    mm.then_inc(m_out.sem, 1)

                def hgrn_attend():
                    pe.wait_ge(m_taken.sem, m_taken.upto(l, 1))
                    for b in range(NB):
                        for h in range(NH):
                            mm = pe.matmul(PS[:, 4 + b, h * P:(h + 1) * P], hsc[:, 2 * b, h, :], vh[:, 0, h * P:(h + 1) * P],
                                           start=True, stop=(b == 0))
                            if b == 1:
                                mm = pe.matmul(PS[:, 4 + b, h * P:(h + 1) * P], hsc[:, 1, h, :], vh[:, 1, h * P:(h + 1) * P],
                                               start=False, stop=True)
                    mm.then_inc(hgrn_out.sem, 1)

                def batch_step(n):
                    def go():
                        if n > 0:
                            attend(n - 1)
                        if n < NBATCH:
                            scores(n)
                    return go

                steps = {}
                steps[0] = conv_weights
                for i in range(NL + 1):
                    steps[LEVEL_STEP[i]] = lambda i=i: level(i)
                steps[LEVEL_STEP[NL] + 1] = gate_turn
                steps[22], steps[23] = turn_q, turn_k
                for n in range(NBATCH + 1):
                    steps[24 + 2 * n] = batch_step(n)
                    if n < NBATCH:
                        steps[25 + 2 * n] = lambda n=n: turn_probs(n)
                steps[37] = spread_m
                steps[38] = lambda: m_scores(0)
                steps[39] = lambda: m_scores(1)
                steps[40] = m_attend
                steps[41] = hgrn_attend

                turn(l, 0, hn)
                for p in range(IN_PIECES):
                    if p % 4 == 0 and p >= 8:
                        pe.wait_ge(drained.sem, drained.upto(l, p // 4 - 1))
                    project(l, p)
                    steps.get(p, nothing)()

                pe.wait_ge(mixed.sem, mixed.upto(l, 1))
                turn(l, 1, hn)
                pe.wait_ge(drained.sem, drained.upto(l, NS))
                for p in range(IN_PIECES, PIECES):
                    o = p // 4 - NS
                    if p % 4 == 0 and o >= 2:
                        pe.wait_ge(out_taken.sem, out_taken.upto(l, o - 1))
                    project(l, p)

                pe.wait_ge(keys_loaded.sem, keys_loaded.upto(l, 2 * HEADS * 16))
                for f in range(4):
                    for i in range(4):
                        mm = pe.transpose(PS[:, 4 + f, i * P:(i + 1) * P], keys[:, 4 * f + i, :], ident)
                    mm.then_inc(keys_turned.sem, 1)
                pe.wait_ge(keys_taken.sem, keys_taken.upto(l, 4))
                turn(l, 2, hn)

                def query(h, s):
                    pe.wait_ge(wq_lo_ready.sem, wq_lo_ready.upto(l, 2 * h + s + 1))
                    w = [m[:].rearrange("p (c n) -> p c n", c=NC).bitcast(F32R) for m in (hi[s], lo[s])]
                    ht = [m[:].bitcast(F32R) for m in hT]
                    for c in range(NC):
                        mm = products(PS[:, 4, s * SEQ:(s + 1) * SEQ], [x[:, c, :] for x in w], [x[:, c, :] for x in ht],
                                      c == 0, c == NC - 1)
                    mm.then_inc(query_done.sem, 1)

                def key_scores(h):
                    pe.wait_ge(query_taken.sem, l * HEADS + h + 1)
                    pe.wait_ge(top_taken.sem, top_taken.upto(l, h * NB))
                    for b in range(NB):
                        for s in range(2):
                            mm = pe.matmul(PS[:, 5, (2 * b + s) * P:(2 * b + s + 1) * P],
                                           qpT[:, s * SEQ + b * P:s * SEQ + (b + 1) * P],
                                           keysT[:, bass.ds(s * HEADS + h, 1), :], start=True, stop=True)
                    mm.then_inc(keyed.sem, 1)

                def sum_rows(h, b, k, last=False):
                    g = h * NB + b
                    if k == 0:
                        pe.wait_ge(sum_taken.sem, sum_taken.upto(l, g))
                    pe.wait_ge(diag_ready.sem, diag_ready.upto(l, (summed(k) if last else g * TOPK + k) + 1))
                    pe.wait_ge(v_loaded[k % RING].sem, ((l * GROUPS + g) * (TOPK // RING) + k // RING) * 16 + 16)
                    for j in range(4):
                        mm = pe.matmul(PS[:, j, :], diag[:, k % RING, :], vrow[k % RING][:, j * 512:(j + 1) * 512],
                                       start=(k == 0), stop=(k == TOPK - 1))
                    mm.then_inc(v_free.sem, 1)

                query(0, 0)
                query(0, 1)
                key_scores(0)
                with pe.Fori(0, HEADS - 1) as h:
                    for k in range(TOPK):
                        sum_rows(h, 0, k)
                        if k in (1, 4):
                            query(h + 1, k // 4)
                        if k == 6:
                            key_scores(h + 1)
                    for k in range(TOPK):
                        sum_rows(h, 1, k)
                for k in range(TOPK):
                    sum_rows(HEADS - 1, 0, k)
                for k in range(TOPK):
                    if k not in VECTOR_SLOTS:
                        sum_rows(HEADS - 1, 1, k, last=True)

        @block.scalar
        def _(act):
            def sumsq(l, use):
                act.activation(rms[:], ones[:, 0:NB], ACT.Sqrt)
                act.wait_ge(x_ready.sem, x_ready.upto(l, use + 1))
                act.activation(hn[:, 0, :], xs[:, 0, :], ACT.Square, accum_out=ss[:, 0:1]).then_inc(sumsq_ready.sem, 1)
                act.wait_ge(var_ready.sem, var_ready.upto(l, use + 1))
                act.activation(rms[:], ss[:], ACT.Sqrt).then_inc(std_ready.sem, 1)

            def take_turned(l, use):
                for f in range(8):
                    act.wait_ge(turned.sem, turned.upto(l, 8 * use + f + 1))
                    g, b = turn_order(use)[f]
                    act.activation(hT[0][:, 4 * g:4 * g + 4, b * P:(b + 1) * P].bitcast(F32R),
                                   bank(4 + f % 4).rearrange("p (c t) -> p c t", c=4), ACT.Copy).then_inc(turned_act.sem, 1)

            act.wait_ge(logits_ready.sem, 1)
            act.activation(lb_all[:, 0].rearrange("p l h -> p (l h)"), lb_all[:, 0].rearrange("p l h -> p (l h)"), ACT.Exp
                           ).then_inc(logits_exped.sem, 1)

            with act.Fori(0, DEPTH) as l:
                done = [0]

                def round_to(n):
                    for p in range(done[0], n):
                        loads = p // RAWS + 1 + min(2, max(0, (p - 4 * KV) // RAWS + 1))
                        act.wait_ge(raw_loaded[p % RAWS].sem, raw_loaded[p % RAWS].upto(l, 16 * loads))
                        if p >= HIS:
                            act.wait_ge(pieces_used.sem, pieces_used.upto(l, p - HIS + 1))
                        elif p == 0:
                            act.wait_ge(query_done.sem, query_done.upto(l, 0))
                        n_ = QC * (SLABS[p // 4][2] if p < IN_PIECES else 512)
                        act.activation(hi[p % HIS][:, 0:n_].bitcast(F32R), raw[p % RAWS][:, 0:n_], ACT.Copy
                                       ).then_inc(hi_ready.sem, 1)
                    done[0] = max(done[0], n)

                def drain(j):
                    round_to(4 * j + 6)
                    act.wait_ge(pieces_used.sem, pieces_used.upto(l, 4 * (j + 1)))
                    name = SLABS[j][0]
                    p = pair(j)
                    pt = p.rearrange("p b (m t) -> p (b m) t", m=2)
                    if name == "fh":
                        act.activation(cum, pt, ACT.Sigmoid)
                        a = act.activation(kk, pt, ACT.Sigmoid, scale=-1.0)
                    elif name == "qh":
                        a = act.activation(silq, pt, ACT.Silu)
                    elif name in ("qa0", "qa1"):
                        c = 512 * int(name[2])
                        a = act.activation(qraw[:, :, c:c + 512], p, ACT.Copy)
                    elif name == "kv":
                        act.activation(gnat[:], p[:, :, 256:256 + 2 * NH], ACT.Copy)
                        a = act.activation(kvraw, p[:, :, 0:256], ACT.Copy)
                    elif name in ("qkm0", "qkm1"):
                        m = 4 * int(name[3])
                        a = act.activation(cin[:, m:m + 4, :], pt, ACT.Copy)
                    elif name == "ih":
                        a = act.activation(vh, p, ACT.Copy)
                    elif name == "vm":
                        a = act.activation(vaug.rearrange("p b h n -> p b (h n)"), p, ACT.Copy)
                    elif name == "gh":
                        a = act.activation(gsilu, p, ACT.Silu)
                    else:
                        a = act.activation(om_sig, p, ACT.Sigmoid)
                    a.then_inc(drained.sem, 1)

                def level_exps(i):
                    round_to(LEVEL_STEP[i] + 1)
                    act.wait_ge(level_diff.sem, level_diff.upto(l, i + 1))
                    w = wts[i % 2]
                    if i < NL:
                        a = act.activation(w, w, ACT.Exp)
                    else:
                        act.activation(w[:, :, 0:P], w[:, :, 0:P], ACT.Exp)
                        a = act.activation(w[:, :, P:SEQ], cum[:, :, P:SEQ], ACT.Exp)
                    a.then_inc(level_exp.sem, 1)

                def batch_exps(n):
                    b, h0, nh = BATCHES[n]
                    round_to(27 + 2 * n)
                    act.wait_ge(masked.sem, masked.upto(l, n + 1))
                    pr = probs.rearrange("p (h s) -> p h s", h=nh)
                    act.activation(esink[:, b, h0:h0 + nh], esink[:, b, h0:h0 + nh], ACT.Exp)
                    for i in range(nh):
                        h = h0 + i
                        a = act.activation(pr[:, i, :], pr[:, i, :], ACT.Exp, bias=nmx[:, b, h:h + 1], scale=DH ** -0.5,
                                           accum_out=rowsum[:, b, h:h + 1])
                    a.then_inc(exped.sem, 1)
                    act.wait_ge(probs_turned.sem, probs_turned.upto(l, n + 1))
                    act.activation(probsT, bank(4, 2), ACT.Copy).then_inc(probs_taken.sem, 1)

                sumsq(l, 0)
                round_to(1)
                take_turned(l, 0)
                drain(0)
                round_to(7)
                act.wait_ge(ln_args.sem, ln_args.upto(l, 1))
                act.activation(cum, cum, ACT.Ln)
                act.activation(wts[0], wts[0], ACT.Ln, scale=1.0 / FLOOR).then_inc(ln_ready.sem, 1)
                drain(1)
                for i in range(5):
                    level_exps(i)
                drain(2)
                for i in range(5, NL + 1):
                    level_exps(i)
                drain(3)
                round_to(21)
                act.wait_ge(softplus_in.sem, softplus_in.upto(l, 1))
                act.activation(rows[0:NH, 5, :], rows[0:NH, 1, :], ACT.Abs)
                act.drain()
                act.activation(rows[0:NH, 5, :], rows[0:NH, 5, :], ACT.Exp, scale=-1.0)
                act.drain()
                act.activation(rows[0:NH, 5, :], rows[0:NH, 5, :], ACT.Ln, bias=1.0).then_inc(softplus_out.sem, 1)
                drain(4)
                round_to(26)
                act.wait_ge(qk_turned.sem, qk_turned.upto(l, 3))
                act.activation(kT.rearrange("p k t -> p (k t)"), bank(4), ACT.Copy).then_inc(qk_taken_act.sem, 1)
                batch_exps(0)
                drain(5)
                batch_exps(1)
                batch_exps(2)
                batch_exps(3)
                drain(6)
                batch_exps(4)
                drain(7)
                batch_exps(5)
                act.wait_ge(conved.sem, conved.upto(l, 4))
                act.activation(cout, cout, ACT.Silu).then_inc(silued.sem, 1)
                round_to(41)
                act.wait_ge(m_exp_in.sem, m_exp_in.upto(l, 1))
                act.activation(mw, mw, ACT.Exp, scale=-1.0)
                act.activation(acol[:, :, 1, :], acol[:, :, 1, :], ACT.Exp).then_inc(m_exp_out.sem, 1)
                drain(8)
                drain(9)
                round_to(45)
                act.wait_ge(hgrn_out.sem, hgrn_out.upto(l, 1))
                act.activation(osq.rearrange("p b h n -> p (b h n)"), bank(4, 2), ACT.Square).then_inc(hgrn_sq.sem, 1)
                act.wait_ge(hgrn_var.sem, hgrn_var.upto(l, 1))
                act.activation(hss[:], hss[:], ACT.Sqrt).then_inc(hgrn_std.sem, 1)
                drain(10)
                take_turned(l, 1)
                round_to(PIECES)

                def round_query(h, s):
                    act.wait_ge(wq_loaded.sem, wq_loaded.upto(l, 16 * (2 * h + s + 1)))
                    act.activation(hi[s][:].bitcast(F32R), raw0[:], ACT.Copy).then_inc(wq_hi_ready.sem, 1)

                act.wait_ge(pieces_used.sem, pieces_used.upto(l, PIECES - 1))
                round_query(0, 0)
                sumsq(l, 1)
                round_query(0, 1)
                for f in range(4):
                    act.wait_ge(keys_turned.sem, keys_turned.upto(l, f + 1))
                    act.activation(keysT[:, 4 * f:4 * f + 4, :].rearrange("p a n -> p (a n)"), bank(4 + f), ACT.Copy
                                   ).then_inc(keys_taken.sem, 1)
                take_turned(l, 2)

                def take_query(h):
                    act.wait_ge(query_done.sem, query_done.upto(l, 2 * h + 2))
                    act.wait_ge(keyed.sem, keyed.upto(l, h))
                    act.activation(qpT, bank(4), ACT.Copy).then_inc(query_taken.sem, 1)

                def gate_exp(h, b):
                    act.wait_ge(tops_ready.sem, l * GROUPS + h * NB + b + 1)
                    act.activation(texp, tops[:], ACT.Exp, bias=gsum[:, 0:1], accum_out=gsum[:, 1:2]).then_inc(gate_exped.sem, 1)

                def gelu(h, b):
                    act.wait_ge(dotted.sem, l * GROUPS + h * NB + b + 1)
                    act.activation(act_k[:, b, :], pre[:, b, :], ACT.Gelu).then_inc(gelued.sem, 1)

                def diagonals(h, b, ks, last=False):
                    g = h * NB + b
                    if ks[0] == 0:
                        act.wait_ge(act_ready.sem, l * GROUPS + g + 1)
                    for k in ks:
                        if last and k in VECTOR_SLOTS:
                            continue
                        n = summed(k - RING) + 1 if last and k >= RING else g * TOPK + k - RING + 1
                        act.wait_ge(v_free.sem, v_free.upto(l, n))
                        act.activation(diag[:, k % RING, :], ident, ACT.Copy, scale=act_k[:, b, k:k + 1]).then_inc(diag_ready.sem, 1)

                take_query(0)
                gate_exp(0, 0)
                gate_exp(0, 1)
                gelu(0, 0)
                with act.Fori(0, HEADS - 1) as h:
                    diagonals(h, 0, range(0, 2))
                    act.wait_ge(query_done.sem, query_done.upto(l, 2 * h + 2))
                    round_query(h + 1, 0)
                    diagonals(h, 0, range(2, 5))
                    round_query(h + 1, 1)
                    diagonals(h, 0, range(5, 7))
                    take_query(h + 1)
                    diagonals(h, 0, range(7, 10))
                    gate_exp(h + 1, 0)
                    diagonals(h, 0, range(10, TOPK))
                    gelu(h, 1)
                    diagonals(h, 1, range(0, 8))
                    gate_exp(h + 1, 1)
                    diagonals(h, 1, range(8, TOPK))
                    gelu(h + 1, 0)
                diagonals(HEADS - 1, 0, range(TOPK))
                gelu(HEADS - 1, 1)
                diagonals(HEADS - 1, 1, range(TOPK), last=True)

            sumsq(DEPTH, 0)

        @block.gpsimd
        def _(pool):
            tables = {"u": peer_u.rearrange("l e d -> (l e) d"), "v": peer_v.rearrange("l e d -> (l e) d")}

            with pool.Fori(0, DEPTH) as l:
                def fetch(kind, h, b, k, last=False):
                    g = h * NB + b
                    idx, free, rows_, loaded = ((idx_u, u_free, urow, u_loaded) if kind == "u"
                                                else (idx_v, v_free, vrow, v_loaded))
                    ready = idx_ready if kind == "u" else vidx_ready
                    if k == 0:
                        pool.wait_ge(ready.sem, ready.upto(l, g + 1))
                    if last and k >= RING and k in VECTOR_SLOTS:
                        stop_until(pool, "pool", v_added.sem, v_added.upto(l, k // RING))
                    else:
                        n = summed(k - RING) + 1 if last and k >= RING else g * TOPK + k - RING + 1
                        stop_until(pool, "pool", free.sem, free.upto(l, n))
                    pool.indirect_dma_start(out=rows_[k % RING], out_offset=None, in_=tables[kind],
                                            in_offset=bass.IndirectOffsetOnAxis(ap=idx[b][:, k:k + 1], axis=0)
                                            ).then_inc(loaded[k % RING].sem, 16)

                for k in range(TOPK):
                    fetch("u", 0, 0, k)
                with pool.Fori(0, HEADS - 1) as h:
                    for k in range(TOPK):
                        fetch("u", h, 1, k)
                        fetch("v", h, 0, k)
                    for k in range(TOPK):
                        fetch("u", h + 1, 0, k)
                        fetch("v", h, 1, k)
                for k in range(TOPK):
                    fetch("u", HEADS - 1, 1, k)
                    fetch("v", HEADS - 1, 0, k)
                for k in range(TOPK):
                    fetch("v", HEADS - 1, 1, k, last=True)

        @block.vector
        def _(dve):
            def bc(ap, shape):
                return ap.to_broadcast(shape)

            for s in (u_free, v_free, gain_used, wq_lo_ready, small_used, top_taken, vidx_ready, sum_taken):
                dve.sem_inc(s.sem, s.start)
            dve.memset(ones[:], 1.0)
            dve.memset(layer_base[:], 0.0)
            dve.wait_ge(const_loaded.sem, 32)
            dve.drain()
            dve.wait_ge(setup_turned.sem, 1)
            z = lb_all[:, 0]
            dve.tensor_copy(z.rearrange("p l h -> p (l h)"), PS[:, 7, 0:DEPTH * NH])
            dve.drain()
            dve.tensor_tensor(lbt[:, 0, :], z[:, 0, :], z[:, 1, :], ALU.max)
            dve.drain()
            for i in range(DEPTH):
                dve.tensor_tensor(z[:, i, :], z[:, i, :], lbt[:, 0, :], ALU.subtract)
            dve.drain().then_inc(logits_ready.sem, 1)
            dve.wait_ge(logits_exped.sem, 1)
            dve.tensor_tensor(lbt[:, 0, :], z[:, 0, :], z[:, 1, :], ALU.add)
            dve.drain()
            dve.reciprocal(lbt[:, 1, :], lbt[:, 0, :])
            dve.drain()
            for i in range(DEPTH):
                dve.tensor_tensor(lbt[:, 2 + i, :], z[:, i, :], lbt[:, 1, :], ALU.mult)
            dve.drain()
            dve.tensor_tensor(lbt[:, 0, :], lbt[:, 2, :], lbt[:, 3, :], ALU.add)
            dve.drain()
            dve.tensor_tensor(z[:, 0, :], lbt[:, 2, :], lbt[:, 2, :], ALU.subtract)
            dve.tensor_tensor(z[:, 1, :], lbt[:, 0, :], lbt[:, 2, :], ALU.subtract)
            dve.drain()
            dve.tensor_scalar(lb_all[:, 1], z, -1.0, 1.0, ALU.mult, ALU.add)
            dve.wait_ge(x_loaded.sem, 16)
            dve.drain().then_inc(x_ready.sem, 1)

            def normalise(l, use):
                dve.tensor_tensor_reduce(hn[:, 1, :], xs[:, 1, :], xs[:, 1, :], 1.0, 0.0, ALU.mult, ALU.add, ss[:, 1:2])
                dve.drain()
                dve.wait_ge(sumsq_ready.sem, sumsq_ready.upto(l, use + 1))
                dve.tensor_scalar(ss[:], ss[:], 1.0 / D, EPS, ALU.mult, ALU.add).then_inc(var_ready.sem, 1)
                dve.wait_ge(std_ready.sem, std_ready.upto(l, use + 1))
                dve.reciprocal(rstd[:], rms[:])
                dve.drain()
                dve.wait_ge(gain_loaded.sem, gain_loaded.upto(l, 16 * (use + 1)))
                for b in range(NB):
                    for c in (slice(0, D // 2), slice(D // 2, D)):
                        dve.scalar_tensor_tensor(out=hn[:, b, c], in0=xs[:, b, c], scalar=rstd[:, b:b + 1], in1=gain[:, c],
                                                 op0=ALU.mult, op1=ALU.mult).then_inc(normed.sem, 1)
                dve.drain().then_inc(gain_used.sem, 1)

            def take_turned(l, use, midway=lambda: None):
                for f in range(8):
                    if f == 1:
                        midway()
                    g, b = turn_order(use)[f]
                    hi_part, lo_part = (h[:, 4 * g:4 * g + 4, b * P:(b + 1) * P] for h in hT)
                    dve.wait_ge(turned_act.sem, turned_act.upto(l, 8 * use + f + 1))
                    dve.tensor_tensor(lo_part.bitcast(F32R), bank(4 + f % 4).rearrange("p (c t) -> p c t", c=4), hi_part, ALU.subtract).then_inc(turned_dve.sem, 1)

            with dve.Fori(0, DEPTH) as l:
                done = [0]

                def split_to(n):
                    for p in range(done[0], n):
                        dve.wait_ge(hi_ready.sem, hi_ready.upto(l, p + 1))
                        if p >= LOS:
                            dve.wait_ge(pieces_used.sem, pieces_used.upto(l, p - LOS + 1))
                        n_ = QC * (SLABS[p // 4][2] if p < IN_PIECES else 512)
                        dve.tensor_tensor(lo[p % LOS][:, 0:n_].bitcast(F32R), raw[p % RAWS][:, 0:n_], hi[p % HIS][:, 0:n_],
                                          ALU.subtract).then_inc(lo_ready.sem, 1)
                    done[0] = max(done[0], n)

                normalise(l, 0)
                take_turned(l, 0, lambda: split_to(1))
                split_to(3)

                dve.wait_ge(small_loaded.sem, small_loaded.upto(l, 4 * 16))
                dve.tensor_scalar(sinks8[:], sinks[:, 0, :], DH ** 0.5, None, ALU.mult)
                dve.tensor_copy(lb[:], lb_all[:, :, bass.ds(l, 1), :].rearrange("p k a h -> p k (a h)"))
                dve.memset(hsc, 0.0)
                dve.wait_ge(conv_turned.sem, conv_turned.upto(l, 1))
                dve.tensor_copy(conv_w[:].rearrange("p j m -> p (j m)"), PS[:, 7, 0:CONV * 2 * NH]).then_inc(conv_ready.sem, 1)

                dve.drain()
                split_to(6)
                dve.wait_ge(drained.sem, drained.upto(l, 1))
                dve.tensor_tensor(kk, kk, bc(lb[:, 1, :].unsqueeze(2), [P, NH, SEQ]), ALU.mult)
                for h in range(NH):
                    dve.tensor_scalar(cum[:, h, :], cum[:, h, :], lb[:, 1, h:h + 1], lb[:, 0, h:h + 1], ALU.mult, ALU.add)
                split_to(7)
                dve.drain()
                dve.tensor_scalar(wts[0], cum, FLOOR, TINY, ALU.min, ALU.max)
                dve.drain()
                dve.tensor_scalar(cum, cum, FLOOR, None, ALU.max)
                dve.drain().then_inc(ln_args.sem, 1)
                split_to(8)
                dve.wait_ge(ln_ready.sem, ln_ready.upto(l, 1))
                dve.tensor_tensor(cum, cum, wts[0], ALU.add)
                dve.drain()
                for h in range(NH):
                    for b in range(NB):
                        r = cum[:, h, b * P:(b + 1) * P]
                        dve.tensor_tensor_scan(r, ones[:], r, 0.0, ALU.mult, ALU.add)
                dve.drain()

                def halves(a, L):
                    a = a.rearrange("p h t -> p (h t)").rearrange("p (g u) -> p g u", u=2 * L)
                    return a[:, :, 0:L], a[:, :, L:2 * L]

                def difference(i):
                    w = wts[i % 2]
                    if i < NL:
                        L = LEVELS[i]
                        (cl, cr), (wl, wr) = halves(cum, L), halves(w, L)
                        m = bc(cl[:, :, L - 1:L], [P, NH * SEQ // (2 * L), L])
                        dve.tensor_tensor(wl, m, cl, ALU.subtract)
                        d = dve.tensor_tensor(wr, cr, m, ALU.subtract)
                    else:
                        d = dve.tensor_tensor(w[:, :, 0:P], bc(cum[:, :, P - 1:P], [P, NH, P]), cum[:, :, 0:P], ALU.subtract)
                    d.then_inc(level_diff.sem, 1)

                def weigh(i):
                    dve.wait_ge(level_exp.sem, level_exp.upto(l, i + 1))
                    if i > 0:
                        dve.wait_ge(level_scored.sem, level_scored.upto(l, min(i, NL)))
                    w = wts[i % 2]
                    if i < NL:
                        L = LEVELS[i]
                        right, left = ([halves(a, L)[r] for a in (o, x, w)] for o, x, r in ((qa_w, silq, 1), (kk_w, kk, 0)))
                    else:
                        right, left = ([a[:, :, t] for a in (o, x, w)]
                                       for o, x, t in ((qa_w, silq, slice(P, SEQ)), (kk_w, kk, slice(0, P))))
                    dve.tensor_tensor(*right, ALU.mult)
                    dve.tensor_tensor(*left, ALU.mult).then_inc(level_ops.sem, 1)

                def take_level(i):
                    split_to(LEVEL_STEP[i] + 3)
                    stop_until(dve, "dve", level_scored.sem, level_scored.upto(l, i + 1))
                    o = hsc[:, 0:2].rearrange("p b h t -> p (b h t)")
                    if i < NL:
                        a, L = CONST["levels"][0] + i * P, LEVELS[i]
                        n = P // (2 * L)
                        m = cst[:, a:a + P].rearrange("p (g u) -> p g u", u=2 * L)[:, :, L:2 * L]
                        m = m.bitcast(I32).unsqueeze(1).to_broadcast([P, NB * NH, n, L])
                        o = o.rearrange("p (x g u) -> p x g u", x=NB * NH, u=2 * L)[:, :, :, L:2 * L]
                        d = PS[:, 4 + i % 2, :].rearrange("p (x g u) -> p x g u", x=NB * NH, u=L)
                    else:
                        m = ident.bitcast(I32).unsqueeze(1).to_broadcast([P, NB * NH, P])
                        o = o.rearrange("p (x t) -> p x t", t=P)
                        d = bank(4, 2).rearrange("p (x t) -> p x t", t=P)
                    dve.copy_predicated(o, m, d)
                    if i == NL:
                        dve.tensor_copy(hsc[:, 2], PS[:, 6, :].rearrange("p (h t) -> p h t", h=NH))
                    dve.drain().then_inc(level_taken.sem, 1)

                dve.memset(kk_w, 0.0)
                difference(0)
                split_to(9)
                dve.wait_ge(drained.sem, drained.upto(l, 2))
                split_to(10)
                for i in range(NL + 1):
                    weigh(i)
                    if i < NL:
                        difference(i + 1)
                        take_level(i)
                    if i == NL - 1:
                        dve.wait_ge(drained.sem, drained.upto(l, 3))
                        dve.tensor_tensor(gnat[:], gnat[:], bc(gate_bias[:], [P, NB, 2 * NH]), ALU.add).then_inc(gates_nat.sem, 1)
                take_level(NL)


                cs = [const(n).rearrange("p (b f) -> p b f", b=NB).unsqueeze(2) for n in ("cos", "sin")]

                def rotate(x1, x2, r1, r2, n, tmp, pieces=0):
                    cos, sin = (bc(c, [P, NB, n, 32]) for c in cs)
                    dve.tensor_tensor(r1, x1, cos, ALU.mult)
                    dve.tensor_tensor(tmp, x2, sin, ALU.mult)
                    dve.tensor_tensor(r2, x2, cos, ALU.mult)
                    dve.drain()
                    dve.tensor_tensor(r1, r1, tmp, ALU.subtract)
                    split_to(pieces)
                    dve.drain()
                    dve.tensor_tensor(tmp, x1, sin, ALU.mult)
                    dve.drain()
                    dve.tensor_tensor(r2, r2, tmp, ALU.add)
                    dve.drain()

                split_to(21)
                dve.wait_ge(gates_turned.sem, gates_turned.upto(l, 1))
                R = [rows[0:NH, r, :] for r in range(6)]
                dve.tensor_copy(rows[0:NH, 0:2, :].rearrange("p r t -> p (r t)"), PS[0:NH, 7, :])
                dve.drain().then_inc(softplus_in.sem, 1)
                dve.wait_ge(softplus_out.sem, softplus_out.upto(l, 1))
                dve.scalar_tensor_tensor(out=R[1], in0=R[1], scalar=0.0, in1=R[5], op0=ALU.min, op1=ALU.subtract)
                dve.drain()
                dve.tensor_tensor_scan(R[5], ones[0:NH, 0:1].to_broadcast([NH, SEQ]), R[1], 0.0, ALU.mult, ALU.add)
                dve.drain()
                dve.tensor_tensor(R[2], R[0], R[5], ALU.subtract)
                dve.drain()
                dve.tensor_tensor_scan(R[3], R[2], R[2], 0.0, ALU.max, ALU.max)
                dve.drain()
                dve.scalar_tensor_tensor(out=R[4], in0=R[5], scalar=-1.0, in1=R[3], op0=ALU.mult, op1=ALU.subtract)
                dve.drain().then_inc(gate_rows.sem, 1)

                split_to(19)
                q5 = qraw.rearrange("p b (h w f) -> p b h w f", h=NQ, w=2)
                r5 = qrot.rearrange("p b (h w f) -> p b h w f", h=NQ, w=2)
                k5 = kvraw[:, :, 0:P].rearrange("p b (h w f) -> p b h w f", h=NKV, w=2)
                o5 = krot[:, :, :, 0, :].rearrange("p b h (w f) -> p b h w f", w=2)
                rotate(k5[:, :, :, 0, :], k5[:, :, :, 1, :], o5[:, :, :, 0, :], o5[:, :, :, 1, :], NKV,
                       rtmp[:, 0:128].rearrange("p (b h f) -> p b h f", b=NB, h=NKV))
                dve.tensor_copy(krot[:, :, :, 1, :], krot[:, :, :, 0, :])
                dve.drain()
                for i in range(2):
                    split_to(22 + i)
                    dve.wait_ge(drained.sem, drained.upto(l, 4 + i))
                    hs = slice(8 * i, 8 * i + 8)
                    rotate(q5[:, :, hs, 0, :], q5[:, :, hs, 1, :], r5[:, :, hs, 0, :], r5[:, :, hs, 1, :], NQ // 2,
                           rtmp.rearrange("p (b h f) -> p b h f", b=NB, h=NQ // 2), 22 + i)
                dve.drain().then_inc(rot_done.sem, 1)

                for i in range(2):
                    split_to(25 + i)
                    dve.wait_ge(qk_turned.sem, qk_turned.upto(l, i + 1))
                    dve.tensor_copy(qT[:, 4 * i:4 * i + 4, :].rearrange("p j t -> p (j t)"), bank(4 + 2 * i, 2)
                                    ).then_inc(qk_taken_dve.sem, 1)

                def soft(n):
                    b, h0, nh = BATCHES[n]
                    hs = slice(h0, h0 + nh)
                    split_to(27 + 2 * n)
                    dve.wait_ge(scored.sem, scored.upto(l, n + 1))
                    m = const("window")[:, 0:2 * P] if b == 1 else const("window")[:, P:2 * P]
                    pr = probs.rearrange("p (h s) -> p h s", h=nh)
                    for r in range(2):
                        dve.tensor_tensor(pr.rearrange("p (j r) s -> p r j s", r=2)[:, r],
                                          PS[:, 6 + r, :].rearrange("p (j s) -> p j s", j=nh // 2),
                                          bc(m.unsqueeze(1), [P, nh // 2, (b + 1) * P]), ALU.add)
                    dve.drain()
                    dve.tensor_reduce(mx[:, b, hs], pr, AX_X, ALU.max)
                    dve.drain()
                    dve.tensor_tensor(mx[:, b, hs], mx[:, b, hs], sinks8[:, hs], ALU.max)
                    dve.drain()
                    dve.tensor_scalar(nmx[:, b, hs], mx[:, b, hs], -DH ** -0.5, None, ALU.mult)
                    dve.drain()
                    dve.tensor_tensor(esink[:, b, hs], nmx[:, b, hs], sinks[:, 0, hs], ALU.add)
                    dve.drain().then_inc(masked.sem, 1)

                def take_probs(n):
                    b, h0, nh = BATCHES[n]
                    hs = slice(h0, h0 + nh)
                    split_to(28 + 2 * n)
                    dve.wait_ge(exped.sem, exped.upto(l, n + 1))
                    dve.tensor_tensor(rinv[:, b, hs], rowsum[:, b, hs], esink[:, b, hs], ALU.add)
                    dve.drain()
                    dve.reciprocal(rinv[:, b, hs], rinv[:, b, hs])
                    dve.drain()

                def take_attended(n):
                    b, h0, nh = BATCHES[n]
                    split_to(29 + 2 * n)
                    dve.wait_ge(attended.sem, attended.upto(l, n + 1))
                    dve.tensor_tensor(hn[:, b, h0 * DH:(h0 + nh) * DH].rearrange("p (h d) -> p h d", h=nh),
                                      PS[:, 4, 0:nh * DH].rearrange("p (h d) -> p h d", h=nh),
                                      bc(rinv[:, b, h0:h0 + nh].unsqueeze(2), [P, nh, DH]), ALU.mult).then_inc(attn_taken.sem, 1)

                def convolve(i):
                    dve.wait_ge(drained.sem, drained.upto(l, 6 + i // 2))
                    tiles = (2 * i, 2 * i + 1)
                    for m in tiles:
                        dve.memset(cout[:, m, 0:CONV - 1], 0.0)
                    for j in range(CONV):
                        s = CONV - 1 - j
                        for m in tiles:
                            w = conv_w[:, j, m:m + 1]
                            if j == 0:
                                dve.tensor_scalar(cout[:, m, s:], cin[:, m, 0:SEQ - s], w, None, ALU.mult)
                            else:
                                dve.scalar_tensor_tensor(out=cout[:, m, s:], in0=cin[:, m, 0:SEQ - s], scalar=w,
                                                         in1=cout[:, m, s:], op0=ALU.mult, op1=ALU.add)
                        d = dve.drain()
                    d.then_inc(conved.sem, 1)

                for n in range(NBATCH):
                    soft(n)
                    if 1 <= n < 5:
                        convolve(n - 1)
                    take_probs(n)
                    take_attended(n)

                split_to(40)
                dve.wait_ge(m_spread.sem, m_spread.upto(l, 1))
                dve.tensor_copy(acol[:].rearrange("p b k h -> p (b k h)"), PS[:, 6, 0:16])
                dve.drain()
                mb = bank(4, 2).rearrange("p (h t) -> p h t", h=NH)
                for h in range(NH):
                    dve.tensor_scalar(mw[:, h, 0:SEQ], mb[:, h, :], acol[:, 0, 0, h:h + 1], 0.0, ALU.subtract, ALU.max)
                    dve.tensor_scalar(mw[:, h, SEQ:SEQ + P], mb[:, h, P:SEQ], acol[:, 1, 0, h:h + 1], 0.0, ALU.subtract, ALU.max)
                dve.drain().then_inc(m_exp_in.sem, 1)
                dve.wait_ge(m_exp_out.sem, m_exp_out.upto(l, 1))
                for a in (0, SEQ):
                    dve.tensor_tensor(mw[:, :, a:a + P], mw[:, :, a:a + P], bc(const("causal").unsqueeze(1), [P, NH, P]), ALU.mult)
                dve.drain()
                for i in range(2):
                    split_to(41 + i)
                    dve.wait_ge(m_scored.sem, m_scored.upto(l, i + 1))
                    base = 6 if i == 0 else 4
                    for j in range(2):
                        dve.scalar_tensor_tensor(out=mp[:, 2 * i + j, :], in0=PS[:, base + j, 0:SEQ + P], scalar=P ** -0.5,
                                                 in1=mw[:, 2 * i + j, :], op0=ALU.mult, op1=ALU.mult)
                dve.drain().then_inc(m_weighted.sem, 1)
                split_to(43)
                dve.wait_ge(m_out.sem, m_out.upto(l, 1))
                dn = den[:].rearrange("p b h -> p (b h)")
                dve.tensor_copy(dn, PS[:, 6, 0:NB * NH])
                dve.drain()
                dve.scalar_tensor_tensor(out=dn, in0=dn, scalar=-1.0, in1=dn, op0=ALU.mult, op1=ALU.max)
                dve.drain()
                dve.tensor_tensor(den[:], den[:], acol[:, :, 1, :], ALU.max)
                dve.drain()
                dve.reciprocal(dn, dn)
                dve.drain()
                ym = hn[:, :, 1536:2048]
                dve.tensor_tensor(ym.rearrange("p b (h n) -> p b h n", h=NH), PS[:, 4:6, :].rearrange("p b (h n) -> p b h n", h=NH),
                                  bc(den[:].unsqueeze(3), [P, NB, NH, P]), ALU.mult)
                dve.drain().then_inc(m_taken.sem, 1)

                dve.wait_ge(drained.sem, drained.upto(l, 10))
                dve.wait_ge(hgain_loaded.sem, hgain_loaded.upto(l, 16))
                dve.tensor_tensor(gsilu, gsilu, bc(hgain, [P, NB, 512]), ALU.mult)
                split_to(44)
                dve.wait_ge(hgrn_sq.sem, hgrn_sq.upto(l, 1))
                dve.tensor_reduce(hss[:], osq, AX_X, ALU.add)
                dve.drain()
                dve.tensor_scalar(hss[:], hss[:], 1.0 / P, EPS, ALU.mult, ALU.add).then_inc(hgrn_var.sem, 1)
                split_to(45)
                dve.wait_ge(hgrn_std.sem, hgrn_std.upto(l, 1))
                dve.reciprocal(hss[:], hss[:])
                dve.drain()
                yh = hn[:, :, 1024:1536]
                dve.tensor_tensor(yh.rearrange("p b (h n) -> p b h n", h=NH), PS[:, 4:6, :].rearrange("p b (h n) -> p b h n", h=NH),
                                  bc(hss[:].unsqueeze(3), [P, NB, NH, P]), ALU.mult)
                dve.drain()
                dve.tensor_tensor(yh, yh, gsilu, ALU.mult)
                dve.drain().then_inc(mixed.sem, 1)
                split_to(46)
                dve.wait_ge(drained.sem, drained.upto(l, NS))
                dve.tensor_tensor(ym, ym, om_sig, ALU.mult)
                dve.drain().then_inc(mixed.sem, 1)
                dve.drain().then_inc(small_used.sem, 1)

                split_to(IN_PIECES + LOS)
                take_turned(l, 1)
                for o in range(NO):
                    split_to(min(PIECES, 4 * (NS + o + 1) + 2))
                    dve.wait_ge(pieces_used.sem, pieces_used.upto(l, 4 * (NS + o + 1)))
                    r = xs[:, :, o * 512:(o + 1) * 512]
                    dve.tensor_tensor(r, r, pair(NS + o), ALU.add).then_inc(out_taken.sem, 1)
                dve.drain().then_inc(x_ready.sem, 1)

                def split_query(h, s):
                    dve.wait_ge(wq_hi_ready.sem, wq_hi_ready.upto(l, 2 * h + s + 1))
                    dve.tensor_tensor(lo[s][:].bitcast(F32R), raw0[:], hi[s][:], ALU.subtract).then_inc(wq_lo_ready.sem, 1)

                split_query(0, 0)
                normalise(l, 1)
                take_turned(l, 2, lambda: split_query(0, 1))

                def top16(vals, idx, src, spare):
                    dve.max(vals[:, 0:8], src)
                    dve.drain()
                    dve.max_index(idx[:, 0:8], vals[:, 0:8], src)
                    dve.match_replace(spare, vals[:, 0:8], src, -3.0e38)
                    dve.drain()
                    dve.max(vals[:, 8:16], spare)
                    dve.drain()
                    dve.max_index(idx[:, 8:16], vals[:, 8:16], spare)

                def choose(h, b):
                    if b == 0:
                        stop_until(dve, "dve", keyed.sem, keyed.upto(l, h + 1))
                    for s in range(2):
                        top16(topv[:, s, :], topi[:, s, :], PS[:, 5, (2 * b + s) * P:(2 * b + s + 1) * P], left[:, s, :])
                    dve.drain().then_inc(top_taken.sem, 1)
                    k3 = [P, TOPK, TOPK]
                    dve.tensor_tensor(cand.rearrange("p (i j) -> p i j", i=TOPK), bc(topv[:, 0, :].unsqueeze(2), k3),
                                      bc(topv[:, 1, :].unsqueeze(1), k3), ALU.add)
                    dve.tensor_copy(topif, topi)
                    dve.drain()
                    top16(tops[:], sel, cand, cand2)
                    dve.drain()
                    dve.tensor_scalar(gsum[:, 0:1], tops[:, 0:1], -1.0, None, ALU.mult).then_inc(tops_ready.sem, 1)
                    dve.tensor_scalar(selhl[:, 0, :], sel, 4, None, ALU.logical_shift_right)
                    dve.tensor_scalar(selhl[:, 1, :], sel, 15, None, ALU.bitwise_and)
                    dve.drain()
                    dve.tensor_copy(selhlf, selhl)
                    dve.drain()
                    for s in range(2):
                        dve.tensor_tensor(hot[:, s], bc(selhlf[:, s, :].unsqueeze(2), k3),
                                          bc(const("iota").unsqueeze(1), k3), ALU.is_equal)
                    dve.drain()
                    for s in range(2):
                        dve.tensor_tensor(hot[:, s], hot[:, s], bc(topif[:, s, :].unsqueeze(1), k3), ALU.mult)
                    dve.drain()
                    dve.tensor_reduce(selidx, hot, AX_X, ALU.add)
                    dve.drain()
                    dve.scalar_tensor_tensor(out=idxf, in0=selidx[:, 0, :], scalar=float(NKEYS), in1=selidx[:, 1, :],
                                             op0=ALU.mult, op1=ALU.add)
                    dve.drain()
                    dve.tensor_scalar(idx_u[b][:], idxf, layer_base[:, 0:1], None, ALU.add)
                    dve.drain().then_inc(idx_ready.sem, 1)
                    dve.wait_ge(gate_exped.sem, l * GROUPS + h * NB + b + 1)
                    dve.reciprocal(gsum[:, 1:2], gsum[:, 1:2])
                    dve.drain()
                    dve.tensor_scalar(gate[:, b, :], texp, gsum[:, 1:2], None, ALU.mult)
                    dve.drain()

                def v_indices(h, b):
                    dve.tensor_copy(idx_v[b][:], idx_u[b][:]).then_inc(vidx_ready.sem, 1)

                def dots(h, b, ks):
                    g = h * NB + b
                    for k in ks:
                        dve.wait_ge(u_loaded[k % RING].sem, ((l * GROUPS + g) * (TOPK // RING) + k // RING) * 16 + 16)
                        r = urow[k % RING]
                        dve.tensor_tensor_reduce(r, r, hn[:, b, :], 1.0, 0.0, ALU.mult, ALU.add, pre[:, b, k:k + 1]
                                                 ).then_inc(u_free.sem, 1)

                def activate(h, b):
                    dve.drain().then_inc(dotted.sem, 1)
                    dve.wait_ge(gelued.sem, l * GROUPS + h * NB + b + 1)
                    dve.tensor_tensor(act_k[:, b, :], act_k[:, b, :], gate[:, b, :], ALU.mult).then_inc(act_ready.sem, 1)

                def take_sum(h, b, last=False):
                    dve.wait_ge(v_free.sem, v_free.upto(l, V_SUMS if last else (h * NB + b + 1) * TOPK))
                    dve.tensor_tensor(xs[:, b, :], xs[:, b, :], bank(0, 4), ALU.add)
                    dve.drain().then_inc(sum_taken.sem, 1)

                def add_row(k):
                    dve.wait_ge(v_loaded[k % RING].sem, ((l * GROUPS + GROUPS - 1) * (TOPK // RING) + k // RING) * 16 + 16)
                    r = xs[:, NB - 1, :]
                    dve.scalar_tensor_tensor(out=r, in0=vrow[k % RING], scalar=act_k[:, NB - 1, k:k + 1], in1=r,
                                             op0=ALU.mult, op1=ALU.add)
                    dve.drain().then_inc(v_added.sem, 1)

                choose(0, 0)
                choose(0, 1)
                v_indices(0, 0)
                dots(0, 0, range(TOPK))
                activate(0, 0)
                with dve.Fori(0, HEADS - 1) as h:
                    dots(h, 1, range(0, 2))
                    split_query(h + 1, 0)
                    dots(h, 1, range(2, 4))
                    split_query(h + 1, 1)
                    dots(h, 1, range(4, 8))
                    choose(h + 1, 0)
                    v_indices(h, 1)
                    dots(h, 1, range(8, TOPK))
                    activate(h, 1)
                    take_sum(h, 0)
                    dots(h + 1, 0, range(0, 6))
                    choose(h + 1, 1)
                    v_indices(h + 1, 0)
                    dots(h + 1, 0, range(6, TOPK))
                    activate(h + 1, 0)
                    take_sum(h, 1)
                v_indices(HEADS - 1, 1)
                dots(HEADS - 1, 1, range(TOPK))
                activate(HEADS - 1, 1)
                take_sum(HEADS - 1, 0)
                for k in VECTOR_SLOTS:
                    add_row(k)
                take_sum(HEADS - 1, 1, last=True)
                dve.tensor_scalar(layer_base[:], layer_base[:], float(EXPERTS), None, ALU.add)
                dve.drain().then_inc(x_ready.sem, 1)

            normalise(DEPTH, 0)


_INS = ["x", "norm_mix", "w_in", "w_out", "attn_sinks", "hgrn_lb_logits", "hgrn_out_norm", "mlstm_conv", "mlstm_i_bias",
        "mlstm_f_bias", "norm_ffn", "peer_query", "peer_sub_keys", "peer_u", "peer_v", "norm_final"]


def kernel(**inputs):
    import numpy as _np
    import concourse.bacc as _bacc
    from concourse import mybir as _mybir
    from concourse.bass_utils import run_bass_kernel_spmd as _run

    nc = _bacc.Bacc("TRN2", target_bir_lowering=False, num_devices=1)
    arrays, args = {}, []
    for name in _INS:
        arrays[f"in_{name}_dram"] = _np.ascontiguousarray(inputs[name])
    arrays["consts_dram"] = constants()
    for name, a in arrays.items():
        args.append(nc.dram_tensor(name, a.shape, _mybir.dt.from_np(a.dtype), kind="ExternalInput").ap())
    out = nc.dram_tensor("out_dram", (1, SEQ, D), F32, kind="ExternalOutput").ap()
    trunk(nc, *args, out)
    r = _run(nc, [arrays], core_ids=[0])
    return r.results[0]["out_dram"]
```
